# Optimizing a Trainium2 kernel written in Bass

```python
import math
import jax, jax.numpy as jnp
from jax import lax
import numpy as np

D_MODEL = 1024
BATCH = 1
SEQ = 256
DEPTH = 1

HEAD_DIM = 64
QBLOCK = 128
EPS = 1e-5
SWA_HEADS = 8
SWA_KV_HEADS = 2
SWA_WINDOW = 128
DIFF_HEADS = 4
NSA_HEADS = 8
NSA_KV_HEADS = 2
CMP_BLOCK = 32
CMP_STRIDE = 16
CMP_HIDDEN = 256
SEL_BLOCK = 64
SEL_TOPN = 16
SEL_QCHUNK = 32
NSA_WINDOW = 512
BRANCH_WIDTH = 512
N_BRANCHES = 3
N_EXPERTS = 32
TOP_K = 4
D_EXPERT = D_MODEL
SWIGLU_LIMIT = 7.0
SWIGLU_ALPHA = 1.702
MOE_BLOCK = 128
A_Q = SWA_HEADS * HEAD_DIM
A_KV = SWA_KV_HEADS * HEAD_DIM
B_QK = DIFF_HEADS * 2 * HEAD_DIM
B_V = DIFF_HEADS * 2 * HEAD_DIM
C_Q = NSA_HEADS * HEAD_DIM
C_KV = NSA_KV_HEADS * HEAD_DIM
NSA_GATES = NSA_HEADS * 3
MERGE_GATES = N_BRANCHES * D_MODEL
IN_SPLITS = (A_Q, A_KV, A_KV, B_QK, B_QK, B_V, C_Q, C_KV, C_KV, C_KV, C_KV, C_KV, C_KV, NSA_GATES, MERGE_GATES)
IN_WIDTH = sum(IN_SPLITS)


def rms_norm(x, g):
    xf = x.astype(jnp.float32)
    y = xf * lax.rsqrt(jnp.mean(xf * xf, axis=-1, keepdims=True) + EPS)
    return (y * g.astype(jnp.float32)).astype(x.dtype)

def alibi_slopes(n):
    return 2.0 ** (-8.0 * jnp.arange(1, n + 1, dtype=jnp.float32) / n)

def banded_attention(q, k, v, window, slopes, sinks=None):
    B, S, Hkv, G, d = q.shape
    nb = S // QBLOCK
    n_prev = -(-(window - 1) // QBLOCK)
    ctx = (n_prev + 1) * QBLOCK
    pad = ((0, 0), (n_prev * QBLOCK, 0), (0, 0), (0, 0))
    kp = jnp.pad(k, pad)
    vp = jnp.pad(v, pad)
    qb = q.reshape(B, nb, QBLOCK, Hkv, G, d).swapaxes(0, 1)
    scale = d ** -0.5

    def block(args):
        qi, i = args
        start = i * QBLOCK
        kc = lax.dynamic_slice_in_dim(kp, start, ctx, axis=1)
        vc = lax.dynamic_slice_in_dim(vp, start, ctx, axis=1)
        s = jnp.einsum('bqhgd,bkhd->bhgqk', qi, kc).astype(jnp.float32) * scale
        t = start + jnp.arange(QBLOCK)
        pos = start - n_prev * QBLOCK + jnp.arange(ctx)
        dist = t[:, None] - pos[None, :]
        valid = (dist >= 0) & (dist < window) & (pos[None, :] >= 0)
        s = s - slopes[:, :, None, None] * dist.astype(jnp.float32)
        s = jnp.where(valid, s, -jnp.inf)
        if sinks is None:
            p = jax.nn.softmax(s, axis=-1)
        else:
            lse = jnp.logaddexp(jax.nn.logsumexp(s, axis=-1, keepdims=True), sinks[:, :, None, None])
            p = jnp.exp(s - lse)
        return jnp.einsum('bhgqk,bkhd->bqhgd', p.astype(vc.dtype), vc)

    o = lax.map(block, (qb, jnp.arange(nb)))
    return o.swapaxes(0, 1).reshape(B, S, Hkv, G, d)

def diff_attention(q, k, v, lam_params, subln_g, slopes, lam_init):
    B, S, H, _, d = q.shape
    nb = S // QBLOCK
    lp = lam_params.astype(jnp.float32)
    lam = jnp.exp(jnp.sum(lp[0] * lp[1])) - jnp.exp(jnp.sum(lp[2] * lp[3])) + lam_init
    qb = q.reshape(B, nb, QBLOCK, H, 2, d).swapaxes(0, 1)
    kpos = jnp.arange(S)
    scale = d ** -0.5

    def block(args):
        qi, i = args
        s = jnp.einsum('bqhcd,bkhcd->bhcqk', qi, k).astype(jnp.float32) * scale
        t = i * QBLOCK + jnp.arange(QBLOCK)
        dist = t[:, None] - kpos[None, :]
        s = s - slopes[:, None, None, None] * dist.astype(jnp.float32)
        s = jnp.where(dist >= 0, s, -jnp.inf)
        p = jax.nn.softmax(s, axis=-1)
        w = p[:, :, 0] - lam * p[:, :, 1]
        return jnp.einsum('bhqk,bkhe->bqhe', w.astype(v.dtype), v)

    o = lax.map(block, (qb, jnp.arange(nb)))
    o = o.swapaxes(0, 1).reshape(B, S, H, 2 * d)
    return rms_norm(o, subln_g) * (1.0 - lam_init)

def compress_blocks(x, pos, w1, b1, w2, b2):
    B, S, Hkv, d = x.shape
    nc = (S - CMP_BLOCK) // CMP_STRIDE + 1
    idx = jnp.arange(nc)[:, None] * CMP_STRIDE + jnp.arange(CMP_BLOCK)[None, :]
    blk = x[:, idx] + pos[:, None, :]
    blk = blk.transpose(0, 1, 3, 2, 4).reshape(B, nc, Hkv, CMP_BLOCK * d)
    hid = jax.nn.gelu(blk @ w1 + b1)
    return hid @ w2 + b2

def nsa_attention(q, k_cmp, v_cmp, k_slc, v_slc, k_win, v_win, gates, cmp_pos, cmp_w1, cmp_b1, cmp_w2, cmp_b2, slopes):
    B, S, Hkv, G, d = q.shape
    scale = d ** -0.5
    t = jnp.arange(S)
    kc = compress_blocks(k_cmp, cmp_pos[0], cmp_w1[0], cmp_b1[0], cmp_w2[0], cmp_b2[0])
    vc = compress_blocks(v_cmp, cmp_pos[1], cmp_w1[1], cmp_b1[1], cmp_w2[1], cmp_b2[1])
    nc = kc.shape[1]
    cstart = jnp.arange(nc) * CMP_STRIDE
    cvalid = (cstart[None, :] + CMP_BLOCK - 1) <= t[:, None]
    s = jnp.einsum('bqhgd,bchd->bhgqc', q, kc).astype(jnp.float32) * scale
    p_cmp = jax.nn.softmax(jnp.where(cvalid, s, -1e30), axis=-1) * cvalid
    o_cmp = jnp.einsum('bhgqc,bchd->bqhgd', p_cmp.astype(vc.dtype), vc)
    nsb = S // SEL_BLOCK
    sstart = jnp.arange(nsb) * SEL_BLOCK
    overlap = jnp.clip(jnp.minimum(cstart[:, None] + CMP_BLOCK, sstart[None, :] + SEL_BLOCK)
                       - jnp.maximum(cstart[:, None], sstart[None, :]), 0).astype(jnp.float32) / CMP_BLOCK
    imp = jnp.einsum('bhgqc,cn->bhqn', p_cmp, overlap)
    cur = t // SEL_BLOCK
    blk = jnp.arange(nsb)
    causal_blk = blk[None, :] <= cur[:, None]
    forced = (blk[None, :] == 0) | (blk[None, :] == cur[:, None]) | (blk[None, :] == cur[:, None] - 1)
    score = jnp.where(forced, jnp.inf, jnp.where(causal_blk, imp, -jnp.inf))
    n_sel = min(SEL_TOPN, nsb)
    top_s, top_i = lax.top_k(score, n_sel)
    sel_ok = top_s > -jnp.inf
    kb = k_slc.reshape(B, nsb, SEL_BLOCK, Hkv, d).transpose(0, 3, 1, 2, 4)
    vb = v_slc.reshape(B, nsb, SEL_BLOCK, Hkv, d).transpose(0, 3, 1, 2, 4)
    nq = S // SEL_QCHUNK
    qch = q.reshape(B, nq, SEL_QCHUNK, Hkv, G, d).swapaxes(0, 1)
    ich = top_i.reshape(B, Hkv, nq, SEL_QCHUNK, n_sel).transpose(2, 0, 1, 3, 4)
    och = sel_ok.reshape(B, Hkv, nq, SEL_QCHUNK, n_sel).transpose(2, 0, 1, 3, 4)
    bidx = jnp.arange(B)[:, None, None, None]
    hidx = jnp.arange(Hkv)[None, :, None, None]

    def chunk(args):
        qi, ii, oki, cidx = args
        kg = kb[bidx, hidx, ii]
        vg = vb[bidx, hidx, ii]
        sc = jnp.einsum('bqhgd,bhqnld->bhgqnl', qi, kg).astype(jnp.float32) * scale
        tq = cidx * SEL_QCHUNK + jnp.arange(SEL_QCHUNK)
        kpos = ii[..., None] * SEL_BLOCK + jnp.arange(SEL_BLOCK)
        dist = tq[None, None, :, None, None] - kpos
        ok = (dist >= 0) & oki[..., None]
        sc = sc - slopes[None, :, :, None, None, None] * dist[:, :, None].astype(jnp.float32)
        sc = jnp.where(ok[:, :, None], sc, -jnp.inf)
        shp = sc.shape
        pr = jax.nn.softmax(sc.reshape(shp[:4] + (shp[4] * shp[5],)), axis=-1).reshape(shp)
        return jnp.einsum('bhgqnl,bhqnld->bqhgd', pr.astype(vg.dtype), vg)

    o_slc = lax.map(chunk, (qch, ich, och, jnp.arange(nq)))
    o_slc = o_slc.swapaxes(0, 1).reshape(B, S, Hkv, G, d)
    o_win = banded_attention(q, k_win, v_win, NSA_WINDOW, slopes)
    g = jax.nn.sigmoid(gates)
    return g[..., 0:1] * o_cmp + g[..., 1:2] * o_slc + g[..., 2:3] * o_win

def hybrid_mixer(h, w_in, b_in, sinks, diff_lambda, diff_subln_g, cmp_pos, cmp_w1, cmp_b1, cmp_w2, cmp_b2, w_branch, w_out, lam_init):
    B, S, _ = h.shape
    z = h @ w_in + b_in
    offs = np.cumsum(IN_SPLITS)[:-1].tolist()
    (qa, ka, va, qb, kb, vb, qc, kcm, vcm, ksl, vsl, kwn, vwn, g_nsa, g_merge) = jnp.split(z, offs, axis=-1)
    ga = SWA_HEADS // SWA_KV_HEADS
    o_a = banded_attention(qa.reshape(B, S, SWA_KV_HEADS, ga, HEAD_DIM),
                           ka.reshape(B, S, SWA_KV_HEADS, HEAD_DIM), va.reshape(B, S, SWA_KV_HEADS, HEAD_DIM),
                           SWA_WINDOW, alibi_slopes(SWA_HEADS).reshape(SWA_KV_HEADS, ga),
                           sinks.astype(jnp.float32).reshape(SWA_KV_HEADS, ga)).reshape(B, S, BRANCH_WIDTH)
    o_b = diff_attention(qb.reshape(B, S, DIFF_HEADS, 2, HEAD_DIM), kb.reshape(B, S, DIFF_HEADS, 2, HEAD_DIM),
                         vb.reshape(B, S, DIFF_HEADS, 2 * HEAD_DIM), diff_lambda, diff_subln_g,
                         alibi_slopes(DIFF_HEADS), lam_init).reshape(B, S, BRANCH_WIDTH)
    gc = NSA_HEADS // NSA_KV_HEADS
    kv = lambda a: a.reshape(B, S, NSA_KV_HEADS, HEAD_DIM)
    o_c = nsa_attention(qc.reshape(B, S, NSA_KV_HEADS, gc, HEAD_DIM), kv(kcm), kv(vcm), kv(ksl), kv(vsl), kv(kwn), kv(vwn),
                        g_nsa.reshape(B, S, NSA_KV_HEADS, gc, 3), cmp_pos, cmp_w1, cmp_b1, cmp_w2, cmp_b2,
                        alibi_slopes(NSA_HEADS).reshape(NSA_KV_HEADS, gc)).reshape(B, S, BRANCH_WIDTH)
    gm = jax.nn.sigmoid(g_merge.reshape(B, S, N_BRANCHES, D_MODEL))
    merged = gm[:, :, 0] * (o_a @ w_branch[0]) + gm[:, :, 1] * (o_b @ w_branch[1]) + gm[:, :, 2] * (o_c @ w_branch[2])
    return merged @ w_out

def moe_ffn(h, router_w, router_b, w1, b1, w2, b2):
    B, S, D = h.shape
    N = B * S
    xt = h.reshape(N, D)
    logits = (xt @ router_w + router_b).astype(jnp.float32)
    top_v, top_e = lax.top_k(logits, TOP_K)
    gate = jax.nn.softmax(top_v, axis=-1)
    A = N * TOP_K
    e_flat = top_e.reshape(A)
    order = jnp.argsort(e_flat)
    e_sorted = e_flat[order]
    tok_sorted = order // TOP_K
    g_sorted = gate.reshape(A)[order]
    counts = jnp.bincount(e_flat, length=N_EXPERTS)
    group_start = jnp.cumsum(counts) - counts
    padded = (counts + MOE_BLOCK - 1) // MOE_BLOCK * MOE_BLOCK
    pad_end = jnp.cumsum(padded)
    pad_start = pad_end - padded
    dest = pad_start[e_sorted] + (jnp.arange(A) - group_start[e_sorted])
    n_blocks = -(-A // MOE_BLOCK) + N_EXPERTS
    P = n_blocks * MOE_BLOCK
    row_tok = jnp.zeros((P,), jnp.int32).at[dest].set(tok_sorted.astype(jnp.int32))
    row_w = jnp.zeros((P,), jnp.float32).at[dest].set(g_sorted)
    block_expert = jnp.clip(jnp.searchsorted(pad_end, jnp.arange(n_blocks) * MOE_BLOCK, side='right'), 0, N_EXPERTS - 1)

    def expert_block(args):
        rows, e = args
        xb = xt[rows]
        hb = xb @ w1[e] + b1[e]
        g, u = hb[:, :D_EXPERT], hb[:, D_EXPERT:]
        g = jnp.minimum(g, SWIGLU_LIMIT)
        u = jnp.clip(u, -SWIGLU_LIMIT, SWIGLU_LIMIT)
        glu = g * jax.nn.sigmoid(g * SWIGLU_ALPHA)
        return ((u + 1.0) * glu) @ w2[e] + b2[e]

    y = lax.map(expert_block, (row_tok.reshape(n_blocks, MOE_BLOCK), block_expert)).reshape(P, D)
    out = jnp.zeros((N, D), y.dtype).at[row_tok].add(y * row_w[:, None].astype(y.dtype))
    return out.reshape(B, S, D)

def first_inputs(seed: int = 0) -> dict:
    key = jax.random.key(seed)
    ks = jax.random.split(key, 32)
    L, D, E, F = DEPTH, D_MODEL, N_EXPERTS, D_EXPERT
    nrm = lambda k, shape, s: jax.random.normal(k, shape, jnp.float32) * s
    return {
        'x': nrm(ks[0], (BATCH, SEQ, D), 1.0),
        'c': nrm(ks[1], (BATCH, D), 1.0),
        'mod_w': nrm(ks[2], (L, D, 6 * D), 0.5 * D ** -0.5),
        'mod_b': nrm(ks[3], (L, 6 * D), 0.02),
        'norm1_g': 1.0 + nrm(ks[4], (L, D), 0.1),
        'norm2_g': 1.0 + nrm(ks[5], (L, D), 0.1),
        'w_in': nrm(ks[6], (L, D, IN_WIDTH), D ** -0.5),
        'b_in': nrm(ks[7], (L, IN_WIDTH), 0.02),
        'sinks': nrm(ks[8], (L, SWA_HEADS), 0.5),
        'diff_lambda': nrm(ks[9], (L, 4, HEAD_DIM), 0.1),
        'diff_subln_g': 1.0 + nrm(ks[10], (L, 2 * HEAD_DIM), 0.1),
        'cmp_pos': nrm(ks[11], (L, 2, CMP_BLOCK, HEAD_DIM), 0.1),
        'cmp_w1': nrm(ks[12], (L, 2, CMP_BLOCK * HEAD_DIM, CMP_HIDDEN), (CMP_BLOCK * HEAD_DIM) ** -0.5),
        'cmp_b1': nrm(ks[13], (L, 2, CMP_HIDDEN), 0.02),
        'cmp_w2': nrm(ks[14], (L, 2, CMP_HIDDEN, HEAD_DIM), CMP_HIDDEN ** -0.5),
        'cmp_b2': nrm(ks[15], (L, 2, HEAD_DIM), 0.02),
        'w_branch': nrm(ks[16], (L, N_BRANCHES, BRANCH_WIDTH, D), BRANCH_WIDTH ** -0.5),
        'w_out': nrm(ks[17], (L, D, D), D ** -0.5),
        'router_w': nrm(ks[18], (L, D, E), D ** -0.5),
        'router_b': nrm(ks[19], (L, E), 0.01),
        'exp_w1': nrm(ks[20], (L, E, D, 2 * F), D ** -0.5),
        'exp_b1': nrm(ks[21], (L, E, 2 * F), 0.02),
        'exp_w2': nrm(ks[22], (L, E, F, D), F ** -0.5),
        'exp_b2': nrm(ks[23], (L, E, D), 0.02),
        'final_g': 1.0 + nrm(ks[24], (D,), 0.1),
    }

def first_block(x, c, mod_w, mod_b, norm1_g, norm2_g, w_in, b_in, sinks, diff_lambda, diff_subln_g, cmp_pos, cmp_w1, cmp_b1, cmp_w2, cmp_b2, w_branch, w_out, router_w, router_b, exp_w1, exp_b1, exp_w2, exp_b2, final_g):
    cs = jax.nn.silu(c)
    for l in range(DEPTH):
        mod = cs @ mod_w[l] + mod_b[l]
        sh1, sc1, g1, sh2, sc2, g2 = [m[:, None, :] for m in jnp.split(mod, 6, axis=-1)]
        lam_init = 0.8 - 0.6 * math.exp(-0.3 * l)
        h = rms_norm(x, norm1_g[l]) * (1.0 + sc1) + sh1
        x = x + g1 * hybrid_mixer(h, w_in[l], b_in[l], sinks[l], diff_lambda[l], diff_subln_g[l], cmp_pos[l], cmp_w1[l],
                                  cmp_b1[l], cmp_w2[l], cmp_b2[l], w_branch[l], w_out[l], lam_init)
        h = rms_norm(x, norm2_g[l]) * (1.0 + sc2) + sh2
        x = x + g2 * moe_ffn(h, router_w[l], router_b[l], exp_w1[l], exp_b1[l], exp_w2[l], exp_b2[l])
    return rms_norm(x, final_g)


DEPTH_2 = 2

RET_HEADS = 4
RET_HEAD_DIM = 128
RET_CHUNK = 128
DSA_HEADS = 8
DSA_HEAD_DIM = 64
DSA_PATTERNS = ((128, 1), (512, 4), (2048, 16))
DSA_BLOCK = 128
T5_BUCKETS = 32
T5_MAX_DIST = 2048
MLSTM_HEADS = 4
MLSTM_HEAD_DIM = 256
MLSTM_CHUNK = 128
MLSTM_CONV = 4
D_FF = 2816
FFN_CONV = 3
LN_EPS = 1e-5
DEEPNORM_ALPHA = (2.0 * DEPTH_2) ** 0.25
DEEPNORM_BETA = (8.0 * DEPTH_2) ** -0.25

N_EVEN = (DEPTH_2 + 1) // 2
N_ODD = DEPTH_2 // 2
RET_W = RET_HEADS * RET_HEAD_DIM
DSA_W = DSA_HEADS * DSA_HEAD_DIM
MIX_W_EVEN = RET_W + DSA_W
EVEN_IN = 4 * RET_W + 3 * DSA_W
EVEN_SPLITS = (RET_W, 2 * RET_W, 3 * RET_W, 4 * RET_W, 4 * RET_W + DSA_W, 4 * RET_W + 2 * DSA_W)
MLSTM_W = MLSTM_HEADS * MLSTM_HEAD_DIM
ODD_IN = 4 * MLSTM_W + 2 * MLSTM_HEADS
ODD_SPLITS = (2 * MLSTM_W, 3 * MLSTM_W, 4 * MLSTM_W)


def layer_norm(x, g, b):
    xf = x.astype(jnp.float32)
    mu = jnp.mean(xf, -1, keepdims=True)
    var = jnp.mean(jnp.square(xf - mu), -1, keepdims=True)
    return ((xf - mu) * lax.rsqrt(var + LN_EPS) * g + b).astype(x.dtype)

def head_norm(y):
    mu = jnp.mean(y, -1, keepdims=True)
    var = jnp.mean(jnp.square(y - mu), -1, keepdims=True)
    return (y - mu) * lax.rsqrt(var + LN_EPS)

def split_heads(t, n_heads):
    B, S, W = t.shape
    return t.reshape(B, S, n_heads, W // n_heads).transpose(0, 2, 1, 3)

def merge_heads(t):
    B, H, S, d = t.shape
    return t.transpose(0, 2, 1, 3).reshape(B, S, H * d)

def causal_dwconv(x, w):
    K, C = w.shape
    return lax.conv_general_dilated(x, w[:, None, :].astype(x.dtype), window_strides=(1,), padding=[(K - 1, 0)], dimension_numbers=("NWC", "WIO", "NWC"), feature_group_count=C)

def rotary(x):
    S, d = x.shape[-2], x.shape[-1]
    inv = 1.0 / (10000.0 ** (jnp.arange(0, d, 2, dtype=jnp.float32) / d))
    ang = jnp.arange(S, dtype=jnp.float32)[:, None] * inv[None, :]
    cos, sin = jnp.cos(ang), jnp.sin(ang)
    x1, x2 = x[..., : d // 2], x[..., d // 2:]
    return jnp.concatenate([x1 * cos - x2 * sin, x1 * sin + x2 * cos], -1)

def retention(q, k, v):
    B, H, S, d = q.shape
    C = RET_CHUNK
    N = S // C
    log_gamma = jnp.log1p(-jnp.exp2(-5.0 - jnp.arange(H, dtype=jnp.float32)))
    qf = rotary(q.astype(jnp.float32))
    kf = rotary(k.astype(jnp.float32)) * (d ** -0.5)
    qc = qf.reshape(B, H, N, C, d)
    kc = kf.reshape(B, H, N, C, d)
    vc = v.astype(jnp.float32).reshape(B, H, N, C, d)
    idx = jnp.arange(C, dtype=jnp.float32)
    rel = idx[:, None] - idx[None, :]
    decay = jnp.where(rel >= 0, jnp.exp(log_gamma[:, None, None] * jnp.maximum(rel, 0.0)), 0.0)
    scores = jnp.einsum('bhncd,bhnsd->bhncs', qc, kc) * decay[None, :, None]
    y_intra = jnp.einsum('bhncs,bhnse->bhnce', scores, vc)
    k_w = jnp.exp(log_gamma[:, None] * (C - 1 - idx)[None, :])
    kv = jnp.einsum('bhnsd,bhnse->bhnde', kc * k_w[None, :, None, :, None], vc)
    chunk_decay = jnp.exp(log_gamma * C)[None, :, None, None]

    def step(R, kv_n):
        return chunk_decay * R + kv_n, R

    _, R_prev = lax.scan(step, jnp.zeros((B, H, d, d), jnp.float32), jnp.moveaxis(kv, 2, 0))
    R_prev = jnp.moveaxis(R_prev, 0, 2)
    q_w = jnp.exp(log_gamma[:, None] * (idx + 1.0)[None, :])
    y_inter = jnp.einsum('bhncd,bhnde->bhnce', qc * q_w[None, :, None, :, None], R_prev)
    return (y_intra + y_inter).reshape(B, H, S, d)

def t5_bucket(dist):
    exact = T5_BUCKETS // 2
    n = jnp.maximum(dist, 0)
    large = exact + (jnp.log(jnp.maximum(n, 1).astype(jnp.float32) / exact) / math.log(T5_MAX_DIST / exact) * (T5_BUCKETS - exact)).astype(jnp.int32)
    large = jnp.minimum(large, T5_BUCKETS - 1)
    return jnp.where(n < exact, n, large)

def dilated_branch(q, k, v, rel_bias, window, dilation):
    B, H, S, d = q.shape
    L = S // dilation
    W = window // dilation
    blk = DSA_BLOCK
    nb = -(-L // blk)
    Lp = nb * blk

    def to_blocks(t):
        t = t.astype(jnp.float32).reshape(B, H, L, dilation, d).swapaxes(2, 3)
        t = jnp.pad(t, ((0, 0), (0, 0), (0, 0), (0, Lp - L), (0, 0)))
        return t.reshape(B, H, dilation, nb, blk, d)

    def with_prev(t):
        prev = jnp.pad(t[:, :, :, :-1], ((0, 0), (0, 0), (0, 0), (1, 0), (0, 0), (0, 0)))
        return jnp.concatenate([prev, t], axis=4)

    qb = to_blocks(q)
    kw = with_prev(to_blocks(k))
    vw = with_prev(to_blocks(v))
    qi = jnp.arange(blk)[:, None] + blk
    kj = jnp.arange(2 * blk)[None, :]
    dist = qi - kj
    bias = rel_bias[t5_bucket(dist * dilation)].astype(jnp.float32).transpose(2, 0, 1)
    blk_start = jnp.arange(nb)[:, None, None] * blk
    valid = (dist >= 0) & (dist <= W) & (blk_start + kj - blk >= 0)
    logits = jnp.einsum('bhrnqd,bhrnkd->bhrnqk', qb, kw) * (d ** -0.5) + bias[None, :, None, None]
    logits = jnp.where(valid, logits, -jnp.inf)
    m = jnp.max(logits, -1)
    p = jnp.exp(logits - m[..., None])
    s = jnp.sum(p, -1)
    o = jnp.einsum('bhrnqk,bhrnkd->bhrnqd', p, vw)

    def from_blocks(t):
        tail = t.shape[5:]
        t = t.reshape((B, H, dilation, Lp) + tail)[:, :, :, :L]
        return jnp.swapaxes(t, 2, 3).reshape((B, H, S) + tail)

    return from_blocks(m), from_blocks(s), from_blocks(o)

def dilated_attention(q, k, v, rel_bias):
    outs = [dilated_branch(q, k, v, rel_bias, w, r) for (w, r) in DSA_PATTERNS]
    M = jnp.max(jnp.stack([m for (m, _, _) in outs]), axis=0)
    num = sum(jnp.exp(m - M)[..., None] * o for (m, _, o) in outs)
    den = sum(jnp.exp(m - M) * s for (m, s, _) in outs)
    return num / den[..., None]

def mlstm(q, k, v, log_i, log_f):
    B, H, S, d = q.shape
    C = MLSTM_CHUNK
    N = S // C
    qc = q.astype(jnp.float32).reshape(B, H, N, C, d)
    kc = (k.astype(jnp.float32) * (d ** -0.5)).reshape(B, H, N, C, d)
    vc = v.astype(jnp.float32).reshape(B, H, N, C, d)
    li = log_i.reshape(B, H, N, C)
    a = jnp.cumsum(log_f.reshape(B, H, N, C), axis=-1)
    g = a[..., -1]
    w_state = g[..., None] - a + li
    m_loc = jnp.max(w_state, -1)
    ew = jnp.exp(w_state - m_loc[..., None])[..., None]
    kv = jnp.einsum('bhncd,bhnce->bhnde', kc * ew, vc)
    ksum = jnp.sum(kc * ew, axis=3)

    def step(carry, inp):
        C_s, n_s, m_s = carry
        kv_n, ks_n, g_n, m_n = inp
        m_new = jnp.maximum(g_n + m_s, m_n)
        a_old = jnp.exp(g_n + m_s - m_new)
        a_loc = jnp.exp(m_n - m_new)
        C_new = a_old[..., None, None] * C_s + a_loc[..., None, None] * kv_n
        n_new = a_old[..., None] * n_s + a_loc[..., None] * ks_n
        return (C_new, n_new, m_new), (C_s, n_s, m_s)

    init = (jnp.zeros((B, H, d, d), jnp.float32), jnp.zeros((B, H, d), jnp.float32), jnp.zeros((B, H), jnp.float32))
    xs = (jnp.moveaxis(kv, 2, 0), jnp.moveaxis(ksum, 2, 0), jnp.moveaxis(g, 2, 0), jnp.moveaxis(m_loc, 2, 0))
    _, (C_prev, n_prev, m_prev) = lax.scan(step, init, xs)
    C_prev = jnp.moveaxis(C_prev, 0, 2)
    n_prev = jnp.moveaxis(n_prev, 0, 2)
    m_prev = jnp.moveaxis(m_prev, 0, 2)
    D = a[..., :, None] - a[..., None, :] + li[..., None, :]
    causal = jnp.tril(jnp.ones((C, C), dtype=bool))
    D = jnp.where(causal, D, -jnp.inf)
    inter_log = a + m_prev[..., None]
    m = jnp.maximum(inter_log, jnp.max(D, -1))
    P = jnp.exp(D - m[..., None]) * jnp.einsum('bhncd,bhnsd->bhncs', qc, kc)
    w_inter = jnp.exp(inter_log - m)
    num = jnp.einsum('bhncs,bhnse->bhnce', P, vc) + w_inter[..., None] * jnp.einsum('bhncd,bhnde->bhnce', qc, C_prev)
    den = jnp.sum(P, -1) + w_inter * jnp.einsum('bhncd,bhnd->bhnc', qc, n_prev)
    h = num / jnp.maximum(jnp.abs(den), jnp.exp(-m))[..., None]
    return h.reshape(B, H, S, d)

def even_mixer(x, w_in, w_out, rel_bias):
    h = x @ w_in
    q_r, k_r, v_r, g_r, q_d, k_d, v_d = jnp.split(h, list(EVEN_SPLITS), axis=-1)
    y_r = retention(split_heads(q_r, RET_HEADS), split_heads(k_r, RET_HEADS), split_heads(v_r, RET_HEADS))
    y_r = merge_heads(head_norm(y_r)) * jax.nn.silu(g_r.astype(jnp.float32))
    y_d = merge_heads(dilated_attention(split_heads(q_d, DSA_HEADS), split_heads(k_d, DSA_HEADS), split_heads(v_d, DSA_HEADS), rel_bias))
    y = jnp.concatenate([y_r, y_d], axis=-1).astype(x.dtype)
    return y @ w_out

def odd_mixer(x, w_in, gate_b, conv_w, w_out):
    h = x @ w_in
    qk, v, o, gates = jnp.split(h, list(ODD_SPLITS), axis=-1)
    qk = jax.nn.silu(causal_dwconv(qk, conv_w))
    q, k = jnp.split(qk, 2, axis=-1)
    gates = gates.astype(jnp.float32) + gate_b
    log_i = gates[..., :MLSTM_HEADS].transpose(0, 2, 1)
    log_f = jax.nn.log_sigmoid(gates[..., MLSTM_HEADS:]).transpose(0, 2, 1)
    y = mlstm(split_heads(q, MLSTM_HEADS), split_heads(k, MLSTM_HEADS), split_heads(v, MLSTM_HEADS), log_i, log_f)
    y = merge_heads(y) * jax.nn.sigmoid(o.astype(jnp.float32))
    return y.astype(x.dtype) @ w_out

def conv_ffn(x, w_up, conv_w, conv_b, w_down):
    gate, up = jnp.split(x @ w_up, 2, axis=-1)
    act = jax.nn.silu(causal_dwconv(gate, conv_w) + conv_b)
    return (act * up) @ w_down

def second_inputs(seed: int = 0) -> dict:
    key = jax.random.key(seed)
    ks = jax.random.split(key, 16)
    f32 = jnp.float32

    def nrm(k, shape, scale):
        return jax.random.normal(k, shape, f32) * scale

    d_in = D_MODEL ** -0.5
    x = nrm(ks[0], (BATCH, SEQ, D_MODEL), 1.0)
    even_scale = np.ones(EVEN_IN, np.float32)
    even_scale[2 * RET_W:3 * RET_W] = DEEPNORM_BETA
    even_scale[4 * RET_W + 2 * DSA_W:] = DEEPNORM_BETA
    even_w_in = nrm(ks[1], (N_EVEN, D_MODEL, EVEN_IN), d_in) * jnp.asarray(even_scale)
    even_w_out = nrm(ks[2], (N_EVEN, MIX_W_EVEN, D_MODEL), MIX_W_EVEN ** -0.5 * DEEPNORM_BETA)
    rel_bias = nrm(ks[3], (T5_BUCKETS, DSA_HEADS), 0.5)
    odd_scale = np.ones(ODD_IN, np.float32)
    odd_scale[2 * MLSTM_W:3 * MLSTM_W] = DEEPNORM_BETA
    odd_w_in = nrm(ks[4], (N_ODD, D_MODEL, ODD_IN), d_in) * jnp.asarray(odd_scale)
    i_bias = nrm(ks[5], (N_ODD, MLSTM_HEADS), 0.1)
    f_bias = jnp.linspace(3.0, 6.0, MLSTM_HEADS, dtype=f32) + nrm(ks[6], (N_ODD, MLSTM_HEADS), 0.1)
    odd_gate_b = jnp.concatenate([i_bias, f_bias], axis=-1)
    odd_conv_w = nrm(ks[7], (N_ODD, MLSTM_CONV, 2 * MLSTM_W), MLSTM_CONV ** -0.5)
    odd_w_out = nrm(ks[8], (N_ODD, MLSTM_W, D_MODEL), MLSTM_W ** -0.5 * DEEPNORM_BETA)
    ffn_w_up = nrm(ks[9], (DEPTH_2, D_MODEL, 2 * D_FF), d_in * DEEPNORM_BETA)
    ffn_conv_w = nrm(ks[10], (DEPTH_2, FFN_CONV, D_FF), FFN_CONV ** -0.5)
    ffn_conv_b = nrm(ks[11], (DEPTH_2, D_FF), 0.02)
    ffn_w_down = nrm(ks[12], (DEPTH_2, D_FF, D_MODEL), D_FF ** -0.5 * DEEPNORM_BETA)
    ln_g = 1.0 + nrm(ks[13], (DEPTH_2, 2, D_MODEL), 0.02)
    ln_b = nrm(ks[14], (DEPTH_2, 2, D_MODEL), 0.02)
    return {"x": x, "even_w_in": even_w_in, "even_w_out": even_w_out, "rel_bias": rel_bias, "odd_w_in": odd_w_in, "odd_gate_b": odd_gate_b, "odd_conv_w": odd_conv_w, "odd_w_out": odd_w_out, "ffn_w_up": ffn_w_up, "ffn_conv_w": ffn_conv_w, "ffn_conv_b": ffn_conv_b, "ffn_w_down": ffn_w_down, "ln_g": ln_g, "ln_b": ln_b}

def second_block(x, even_w_in, even_w_out, rel_bias, odd_w_in, odd_gate_b, odd_conv_w, odd_w_out, ffn_w_up, ffn_conv_w, ffn_conv_b, ffn_w_down, ln_g, ln_b):
    for layer in range(DEPTH_2):
        j = layer // 2
        if layer % 2 == 0:
            mix = even_mixer(x, even_w_in[j], even_w_out[j], rel_bias)
        else:
            mix = odd_mixer(x, odd_w_in[j], odd_gate_b[j], odd_conv_w[j], odd_w_out[j])
        x = layer_norm(DEEPNORM_ALPHA * x + mix, ln_g[layer, 0], ln_b[layer, 0])
        ffn = conv_ffn(x, ffn_w_up[layer], ffn_conv_w[layer], ffn_conv_b[layer], ffn_w_down[layer])
        x = layer_norm(DEEPNORM_ALPHA * x + ffn, ln_g[layer, 1], ln_b[layer, 1])
    return x


def setup_inputs(seed=0):
    out = dict(first_inputs(seed))
    for name, value in second_inputs(seed + 1).items():
        if name != "x":
            out[name + "_2"] = value
    return out


def reference(
    x, c, mod_w, mod_b, norm1_g, norm2_g, w_in, b_in, sinks, diff_lambda, diff_subln_g, cmp_pos,
    cmp_w1, cmp_b1, cmp_w2, cmp_b2, w_branch, w_out, router_w, router_b, exp_w1, exp_b1, exp_w2,
    exp_b2, final_g, even_w_in_2, even_w_out_2, rel_bias_2, odd_w_in_2, odd_gate_b_2,
    odd_conv_w_2, odd_w_out_2, ffn_w_up_2, ffn_conv_w_2, ffn_conv_b_2, ffn_w_down_2, ln_g_2,
    ln_b_2,
):
    x = first_block(
        x, c, mod_w, mod_b, norm1_g, norm2_g, w_in, b_in, sinks, diff_lambda, diff_subln_g,
        cmp_pos, cmp_w1, cmp_b1, cmp_w2, cmp_b2, w_branch, w_out, router_w, router_b, exp_w1,
        exp_b1, exp_w2, exp_b2, final_g,
    )
    return second_block(
        x, even_w_in_2, even_w_out_2, rel_bias_2, odd_w_in_2, odd_gate_b_2, odd_conv_w_2,
        odd_w_out_2, ffn_w_up_2, ffn_conv_w_2, ffn_conv_b_2, ffn_w_down_2, ln_g_2, ln_b_2,
    )


_drawn_inputs = setup_inputs


def setup_inputs(seed=0):
    import zlib

    import numpy as np

    out = dict(_drawn_inputs(seed))
    spreads = {}
    factors = {'b_in': 3.822,
     'sinks': 7.665,
     'diff_lambda': 5.752,
     'diff_subln_g': 2.795,
     'cmp_pos': 6.366,
     'cmp_b1': 33.211,
     'cmp_b2': 26.801,
     'router_b': 3.969,
     'exp_b1': 8.0,
     'exp_b2': 8.0,
     'rel_bias_2': 5.48,
     'odd_conv_w_2': 37.848,
     'ffn_conv_b_2': 8.0}
    for name, (base, spread) in spreads.items():
        noise = np.random.default_rng([zlib.crc32(name.encode()), seed]).standard_normal(out[name].shape)
        drawn = base * np.exp(spread * noise) if base else spread * noise
        out[name] = __import__('jax').numpy.asarray(drawn.astype(out[name].dtype))
    for name, factor in factors.items():
        out[name] = (out[name] * factor).astype(out[name].dtype)
    return out
```

```python
import math
from contextlib import ExitStack

import numpy as np
import concourse.bass as bass
from concourse import mybir

F32 = mybir.dt.float32
I32 = mybir.dt.int32
U32 = mybir.dt.uint32
ALU = mybir.AluOpType
ACT = mybir.ActivationFunctionType
AX = mybir.AxisListType

P = 128
T = 256
NT = T // P
D = 1024
KD = D // P
HD = 64
NEG = -1.0e30
EPS = 1e-5
N_EXP = 32
TOP_K = 4
W1_ORDER = (2, 3, 4, 5, 6, 7, 0, 1)
SLOTS = 64
D_FF = 2816
NF = D_FF // P
ALPHA = (2.0 * 2) ** 0.25
LAM_INIT = 0.8 - 0.6 * math.exp(-0.3 * 0)

A_Q0, A_K0, A_V0 = 0, 512, 640
B_Q0, B_K0, B_V0 = 768, 1280, 1792
C_Q0, C_KCMP0, C_VCMP0, C_KSEL0, C_VSEL0, C_KWIN0, C_VWIN0 = 2304, 2816, 2944, 3072, 3200, 3328, 3456
NSA_G0, MERGE0 = 3584, 3608
IN_W = 6680

CA = {}
CS = {}
CB = {}


def _lay(table, *items):
    at = 0
    for name, n in items:
        table[name] = (at, n)
        at += n
    return at


NCA = _lay(CA, ("ident", 128), ("ones", 128), ("tri", 128), ("iota", 256), ("cmp_add", 256),
           ("cmp_valid", 256), ("cmp_rep", 256), ("cmp_head", 8), ("token_id", 2), ("tri_incl", 128))
NCS = _lay(CS, ("dist", 384), ("causal", 384), ("window", 128))
NCB = _lay(CB, ("cos", 256), ("sin", 256), ("swap", 128), ("decay", 4 * 384), ("log_mult", 384),
           ("causal_b", 384), ("head_sel", 4 * 128))

ROW_C, ROW_N1, ROW_N2, ROW_B = 0, 8, 16, 24
BI_QA, BI_KA, BI_QB, BI_KB, BI_QC, BI_KCMP, BI_VCMP, BI_KSEL, BI_KWIN, BI_GATE = 0, 4, 5, 9, 13, 17, 19, 21, 22, 23
ROW_SUB = ROW_B + 47
ROW_B2 = ROW_SUB + 1
ROW_POS = ROW_B2 + 1
ROW_FG = ROW_POS + 32
N_ROWS = ROW_FG + 8
N_FROWS = 4 * NF
COL_F = (N_ROWS, N_ROWS + N_FROWS)
COL_O = N_ROWS + 2 * N_FROWS
N_ROWS_O = 64
COL_LNG, COL_LNB = COL_O + N_ROWS_O, COL_O + N_ROWS_O + 32
N_COLS = COL_LNB + 32


def shape_constants():
    f = np.float32
    ca = np.zeros((P, NCA), f)
    cs = np.zeros((P, NCS), f)
    cb = np.zeros((P, NCB), f)
    p = np.arange(P)

    def put(arr, table, name, value):
        at, n = table[name]
        value = np.asarray(value, f)
        arr[: value.shape[0], at:at + n] = value.reshape(value.shape[0], n)

    put(ca, CA, "ident", np.eye(P))
    put(ca, CA, "ones", np.ones((P, P)))
    put(ca, CA, "tri", p[:, None] < p[None, :])
    put(ca, CA, "tri_incl", p[:, None] <= p[None, :])
    put(ca, CA, "iota", np.tile(np.arange(T), (P, 1)))
    rel = np.concatenate([p[:, None] - p[None, :], p[:, None] + P - np.arange(T)[None, :]], 1)
    put(cs, CS, "dist", -rel)
    put(cs, CS, "causal", np.where(rel >= 0, 0.0, NEG))
    put(cs, CS, "window", np.where(rel[:, 128:256] < 128, 0.0, NEG))
    nc_blocks = (T - 32) // 16 + 1
    ends = np.arange(16) * 16 + 31
    t = np.arange(T).reshape(NT, P).T
    valid = (ends[None, None, :] <= t[:, :, None]) & (np.arange(16) < nc_blocks)
    valid = np.broadcast_to(valid[:, :, None, :], (P, NT, 8, 16))
    pad = np.broadcast_to(np.arange(16) >= nc_blocks, valid.shape)
    put(ca, CA, "cmp_add", np.where(pad, 3 * NEG, np.where(valid, 0.0, NEG)))
    put(ca, CA, "cmp_valid", valid)
    rep = np.zeros((16, 2, P))
    for h in range(8):
        for c in range(nc_blocks):
            rep[c, h // 4, h * 16 + c] = 1
    put(ca, CA, "cmp_rep", rep)
    head = np.zeros((P, 8))
    head[p, p // 16] = 1
    put(ca, CA, "cmp_head", head)
    put(ca, CA, "token_id", t)

    inv = (f(1.0) / (f(10000.0) ** (np.arange(0, 128, 2, dtype=f) / f(128)))).astype(f)
    ang = (np.arange(T, dtype=f)[:, None] * inv[None, :]).astype(f)
    cos, sin = np.cos(ang).T, np.sin(ang).T
    put(cb, CB, "cos", np.concatenate([cos, cos], 0))
    put(cb, CB, "sin", np.concatenate([-sin, sin], 0))
    put(cb, CB, "swap", np.eye(P)[(p + 64) % P])
    lg = np.log1p(-np.exp2(-5.0 - np.arange(4.0)))
    k0 = np.arange(T)[None, :] - p[:, None]
    relt = np.concatenate([k0, k0[:, :128]], 1)
    decay = np.where(relt >= 0, np.exp(lg[:, None, None] * np.maximum(relt, 0)), 0.0) * 128 ** -0.5
    put(cb, CB, "decay", decay.transpose(1, 0, 2))
    mult = (rel >= 0) * ((rel <= 128) * 1.0 + (rel % 4 == 0) + (rel % 16 == 0))
    put(cb, CB, "log_mult", np.where(mult > 0, np.log(np.maximum(mult, 1)), NEG))
    put(cb, CB, "causal_b", np.where(rel >= 0, 0.0, NEG))
    sel = np.zeros((4, 4, P))
    for h in range(4):
        sel[h, h] = 1
    put(cb, CB, "head_sel", sel)

    dist = np.maximum(255 - np.arange(384), 0)
    large = 16 + (np.log(np.maximum(dist, 1).astype(f) / f(16)) / f(math.log(2048 / 16)) * f(16)).astype(np.int32)
    bucket = np.where(dist < 16, dist, np.minimum(large, 31))
    onehot = (np.arange(32)[:, None] == bucket[None, :]).astype(f)
    return ca, cs, cb, onehot


class Tally:

    def __init__(self, sem):
        self.sem, self.n = sem, 0

    def add(self, instruction):
        instruction.then_inc(self.sem, 1)
        self.n += 1
        return instruction


class Arena:

    def __init__(self, tensor, columns):
        self.t, self.columns, self.at, self.most = tensor, columns, 0, 0

    def take(self, n, *inner):
        v = self.view(self.at, n, *inner)
        self.at += n
        self.most = max(self.most, self.at)
        assert self.at <= self.columns, (self.at, self.columns)
        return v

    def view(self, at, n, *inner):
        v = self.t[:, at:at + n]
        if len(inner) == 1:
            return v.rearrange("p (a b) -> p a b", b=inner[0])
        if len(inner) == 2:
            return v.rearrange("p (a b c) -> p a b c", b=inner[0], c=inner[1])
        return v


def program(nc, a, out, debug=None):
    ctx = ExitStack()
    with ctx:
        def sem(name):
            return ctx.enter_context(nc.semaphore(name))

        columns = 53208
        arena = Arena(ctx.enter_context(nc.sbuf_tensor("arena", [P, columns], F32)), columns)
        psum = ctx.enter_context(nc.psum_tensor("psum", [P, 8 * 512], F32))
        bank = [psum[:, 512 * i:512 * i + 512] for i in range(8)]
        scratch = nc.dram_tensor("bias_rows", (8, P, 384), F32).ap()
        score_banks = psum[:, 1024:2048].rearrange("p (h n) -> p h n", h=2)

        const = arena.take(NCA)
        cols = arena.take(N_COLS)
        x_res = arena.take(NT * D, D)
        g2b = arena.take(D)
        stat = arena.take(640)

        def ca(name):
            at, n = CA[name]
            return const[:, at:at + n]

        ident, ones, iota = ca("ident"), ca("ones"), ca("iota")
        cmp_rep = ca("cmp_rep").rearrange("p (g n) -> p g n", g=2)
        cmp_head = ca("cmp_head")
        mod = stat[:, 0:48]
        silu_c = stat[:, 48:56]
        scale1, scale2 = stat[:, 56:64], stat[:, 64:72]
        lam_neg = stat[:, 72:73]
        nsink = stat[:, 80:88]
        sinks = stat[:, 88:96]
        unit_stat = stat[:, 96:96 + 3 * 80].rearrange("p (s u) -> p s u", s=3)
        misc = stat[:, 336:640]
        lam_row = misc[:, 0:256]
        lam_sum = misc[:, 256:262]
        sumsq = misc[:, 264:266]
        rstd = misc[:, 266:268]
        sub_stat = misc[:, 268:276]
        phase = arena.at

        ring = [arena.take(4096) for _ in range(4)]
        at_ht = arena.at
        hT = arena.take(KD * T, T)
        at_mod = arena.at
        modrow = arena.take(3 * 512, 512)
        at_qa = arena.at
        qaT, kaT = arena.take(1024, T), arena.take(256)
        at_qb = arena.at
        qbT, kbT = arena.take(1024, T), arena.take(1024, T)
        at_qc = arena.at
        qcT, kselT, kwinT = arena.take(1024, T), arena.take(256), arena.take(256)
        at_e = arena.at
        shifted = arena.take(4 * T, T)
        cmp_in = arena.take(2 * 16 * 32, 16, 32)
        vtok = arena.take(NT * 896, 896)
        at_gate = arena.at
        gateT = arena.take(24 * T, T)
        oT = [arena.take(1024, T) for _ in range(3)]
        alibi = arena.take(8 * 384, 384)
        score_sb = arena.take(1024)
        prob = arena.take(1024)
        probT_sb = arena.take(1024)
        hid, hid_t = arena.take(256), arena.take(256)
        hidT = arena.take(128, 64)
        kcT, vcT = arena.take(16), arena.take(128, 64)
        vz, vrep = arena.take(512, 64), arena.take(64)
        cmp_s, probT_cmp = arena.take(256), arena.take(256)
        cmp_stat = arena.take(48)
        cmp_w2 = arena.take(256, 64)
        cmp_b1 = arena.take(512)
        cmp_b2v = arena.take(64)
        nsa_g = arena.take(48, 24)
        mixer_end = arena.at
        xn = arena.view(at_e, 2048, D)
        mergedT = arena.view(at_qb, 2048, T)
        g1b = arena.view(at_qc, 1024)
        start_const = arena.view(at_gate, NCS)
        b_row = arena.view(at_gate + NCS, 920)
        alibi_w = arena.view(at_gate + 4096, 2048, 256)
        rows = arena.view(at_gate + 2048, 512, P)
        o_tok = arena.view(at_qa, 1024, 512)
        silu32 = g2b[:, 0:256].rearrange("p (k n) -> p k n", k=8)

        w1 = [arena.view(phase + 2048 * k, 2048) for k in range(KD)]
        w2 = [arena.view(at_e + 1024 * k, 1024) for k in range(KD)]
        arena.at = at_ht
        exp_b2, router_w, router_b = arena.take(1024), arena.take(256, 32), arena.take(32)
        exp_b1 = arena.take(512)
        arena.at = at_mod
        xn2 = arena.take(2048, D)
        h2T = arena.take(2048, T)
        arena.at = at_qc
        xgT = arena.take(1024, P)
        arena.at = at_e + KD * 1024
        logits = arena.take(64, 32)
        best = arena.take(16, 8)
        best_at_int, best_at = arena.take(16, 8), arena.take(16, 8)
        top_gate = arena.take(8, 4)
        top_stat = arena.take(8)
        onehots = arena.take(256, 4, 32)
        chosen, gates_t = arena.take(64, 32), arena.take(64, 32)
        slot_of = arena.take(2 * (N_EXP + 1), N_EXP + 1)
        id_gate = arena.take(NT * (N_EXP + 1) * 2, N_EXP + 1, 2)
        counts, passes = arena.take(N_EXP + 1), arena.take(3 * N_EXP, N_EXP)
        counts_int, before_int = arena.take(N_EXP), arena.take(N_EXP)
        counts_int_i, before_int_i = counts_int.bitcast(I32), before_int.bitcast(I32)
        gatesT = arena.take(T)
        slot_data, slot_data_ov, expert_data = arena.take(2), arena.take(2), arena.take(2 * NT, 2)
        select = arena.take(NT * P, P)
        spreadT, spreadT_ov = arena.take(T), arena.take(T)
        select_ov, xgT_ov = arena.take(NT * SLOTS, SLOTS), arena.take(KD * SLOTS, SLOTS)
        gate_part, up_part, gate_tanh, hidden = (arena.take(512) for _ in range(4))
        hiddenT, y_sb, y_ov = arena.take(512, P), arena.take(512), arena.take(512)

        vectors_at = at_gate + 12288 - 784
        assert arena.at <= vectors_at
        arena.at = vectors_at
        rel_bias, rel_onehot, bias_row = arena.take(8), arena.take(384), arena.take(384)
        gate_b = arena.take(8)
        assert arena.at <= at_gate + 12288
        cb = arena.view(at_gate + 12288 + 3072, NCB)
        arena.at = at_ht
        xT, z, yT = arena.take(2048, T), arena.take(2048, D), arena.take(2048, T)
        toep = arena.take(8 * 384, 384)
        final_gb = toep.rearrange("p a b -> p (a b)")[:, 0:2048].rearrange("p (a b) -> p a b", a=2)
        alpha_ident = arena.take(P)
        ln_bn, ln_mv = arena.take(4 * 6, 6), arena.take(4, 2)
        at_b = arena.at
        raw, rot = arena.take(2048, T), arena.take(2048, T)
        v_r, v_d = arena.take(1024, 512), arena.take(1024, 512)
        qdT, kdT = arena.take(1024, T), arena.take(1024, T)
        decayed = arena.take(4 * 384, 384)
        y_even, g_raw, g_tanh = arena.take(1024, 512), arena.take(1024, 512), arena.take(1024, 512)
        rot_sin = arena.take(256)
        ret_bn, ret_mv = arena.take(8 * 6, 6), arena.take(8 * 2, 2)
        assert arena.at <= vectors_at
        arena.at = at_b
        qkT, v_o, o_tanh = arena.take(4096, T), arena.take(2048, D), arena.take(2048, D)
        expD, y_odd = arena.take(4 * 384, 384), arena.take(2048, D)
        conv_acc, conv_t = arena.take(512, 256), arena.take(512, 256)
        gates_o, log_f, cum_f, low_i = arena.take(16, 8), arena.take(8, 4), arena.take(8, 4), arena.take(8, 4)
        neg_r, floor_e, den_r = arena.take(8, 4), arena.take(8, 4), arena.take(8)
        low_iT = arena.take(256)
        assert arena.at <= vectors_at
        arena.at = at_b
        ffn_z, ffn_t, ffn_h = arena.take(512, 256), arena.take(512, 256), arena.take(512, 256)

        def cbc(name):
            at, n = CB[name]
            return cb[:, at:at + n]

        def csc(name):
            at, n = CS[name]
            return start_const[:, at:at + n]

        panels, jobs = [], []

        def panel(kind, *rest):
            panels.append((kind, *rest))
            return len(panels) - 1

        def job(kind, engine, q, **more):
            jobs.append(dict(kind=kind, engine=engine, panels=q, **more))
            return len(jobs) - 1

        def feature(q, starts, dest, bias):
            return job("feature", "act", [q], starts=[s - panels[q][1] for s in starts], dest=dest, bias=bias)

        def token(q, start, n, dest, row, gates=False):
            for i in range(NT):
                job("token", "dve", [q], start=start - panels[q][1], n=n, tile=i, dest=dest, row=row, gates=gates)

        mod0 = [panel("mod", 0, c) for c in range(4)]
        q_a = panel("in", 0, 512)
        for j in range(4):
            feature(q_a, (A_Q0 + 64 * j, A_Q0 + 256 + 64 * j), qaT[:, j, :], BI_QA + j)
        q_ab = panel("in", 512, 512)
        feature(q_ab, (A_K0,), kaT, BI_KA)
        token(q_ab, A_V0, 128, 0, 0)
        first_a = len(jobs)
        feature(q_ab, (B_Q0,), qbT[:, 0, :], BI_QB)
        feature(q_ab, (B_Q0 + 128,), qbT[:, 1, :], BI_QB + 1)
        q = panel("in", 1024, 512)
        for j in (2, 3):
            feature(q, (B_Q0 + 128 * j,), qbT[:, j, :], BI_QB + j)
        for j in (0, 1):
            feature(q, (B_K0 + 128 * j,), kbT[:, j, :], BI_KB + j)
        q = panel("in", 1536, 512)
        for j in (2, 3):
            feature(q, (B_K0 + 128 * j,), kbT[:, j, :], BI_KB + j)
        token(q, B_V0, 256, 128, 128)
        q = panel("in", 2048, 256)
        token(q, 2048, 256, 384, 384)
        first_b = len(jobs)
        q = panel("in", C_Q0, 512)
        for j in range(4):
            feature(q, (C_Q0 + 64 * j, C_Q0 + 256 + 64 * j), qcT[:, j, :], BI_QC + j)
        q = panel("in", C_KCMP0, 512)
        for n in range(4):
            at = C_KCMP0 + 64 * n
            job_last_shift = job("shifted", "act", [q], starts=[at - C_KCMP0, at - C_KCMP0], dest=shifted[:, n, :], bias=BI_KCMP + n)
        feature(q, (C_KSEL0,), kselT, BI_KSEL)
        token(q, C_VSEL0, 128, 640, 640)
        q = panel("in", C_KWIN0, 280)
        feature(q, (C_KWIN0,), kwinT, BI_KWIN)
        token(q, C_VWIN0, 152, 768, 768, gates=True)
        job_gates = len(jobs) - 1
        q_w1 = [panel("cmp", n) for n in range(2)]
        job_hid = job("cmp_hidden", "dve", q_w1)
        job("cmp_hidden_t", "act", [])
        job("cmp_k", "act", [])
        job("cmp_v", "act", [])
        job("cmp_v_rep", "dve", [])
        job_cmp_qk = job("cmp_scores", "dve", [])
        job_cmp_t = job("cmp_prob_t", "act", [])
        first_c = len(jobs)
        for n in range(6):
            q = panel("in", MERGE0 + 512 * n, 512)
            for m in range(4):
                b = 4 * n + m
                job("gate", "act", [q], starts=[128 * m], dest=gateT[:, b, :], bias=BI_GATE + b)
        for g in (1, 2):
            qs = [panel("mod", g, c) for c in range(4)]
            job("mod", "dve", qs, group=g)
            job("mod_t", "dve", [], group=g)
        job_g1 = job("broadcast", "act", [], row=0, group=1, dest=g1b[:, 0:512], factor=0.5)
        job("broadcast", "act", [], row=1, group=1, dest=g1b[:, 512:1024], factor=0.5)
        job("broadcast", "act", [], row=2, group=2, dest=g2b[:, 0:512], factor=1.0)
        job("broadcast", "act", [], row=3, group=2, dest=g2b[:, 512:1024], factor=1.0)
        last_gate = max(n for n, jb in enumerate(jobs) if jb["kind"] == "gate")
        steps_end = len(jobs)
        job_ob = [job("diff_out_t", "act", [], head=h) for h in range(4)]
        q_b = [panel("branch", n) for n in range(3)]
        for k in range(KD):
            for br in range(3):
                job("branch", "dve", q_b if k == KD - 1 else [], chunk=k, branch=br)
        q_o = [panel("out", n) for n in range(2)]
        for n in range(2):
            for i in range(NT):
                job("mix_out", "dve", [q_o[n]], half=n, tile=i)
        n_jobs = len(jobs)

        n_panels = len(panels)

        def turned_x(g, b):
            return [job("xt", ("act", "dve")[q % 2], [], quarter=q, g=g, b=b) for q in range(4)]

        def mix_jobs(name):
            q_w = [panel(name, n) for n in range(2)]
            turned_jobs = [len(jobs) - 1, len(jobs) - 2]
            for i in range(NT):
                for half in range(2):
                    job("mix_out_b", "act", [q_w[half]], half=half, tile=i, dest=z[:, i, 512 * half:512 * half + 512],
                        n=512, after=turned_jobs if i == half == 0 else [])
            return len(jobs) - 4

        job_xt0 = turned_x(ROW_FG, None)
        q_d, k_d, v_dp = (panel("even_in", c, 512) for c in (2048, 2560, 3072))
        for m in range(4):
            job("b_feature", "act", [q_d], start=P * m, dest=qdT[:, m, :], after=job_xt0[2:] if m == 0 else [])
        for m in range(4):
            job("b_feature", "act", [k_d], start=P * m, dest=kdT[:, m, :])
        for i in range(NT):
            job("b_token", "dve", [v_dp], tile=i, start=0, n=512, dest=v_d[:, i, :])
        first_even = len(jobs)
        q_r, k_r, v_rp, g_rp = (panel("even_in", c, 512) for c in (0, 512, 1024, 1536))
        raw_jobs = []
        for m in range(8):
            raw_jobs.append(job("b_feature", "act", [(q_r, k_r)[m // 4]], start=P * (m % 4), dest=raw[:, m, :]))
            if m >= 1:
                job("swap", "dve", [], m=m - 1, after=[raw_jobs[m - 1]])
        for i in range(NT):
            job("b_token", "dve", [v_rp], tile=i, start=0, n=512, dest=v_r[:, i, :])
            if i == 0:
                job("swap", "dve", [], m=7, after=[raw_jobs[7]])
        job_rv = []
        job_rs = []
        for h in range(5):
            if h < 4:
                job_rs.append(job("ret_scores", "dve", [], head=h, after=[len(jobs) - 1] if h == 0 else []))
            if h >= 1:
                job_rv.append(job("ret_value", "act", [], head=h - 1, after=[job_rs[h - 1]],
                                  dest=y_even[:, :, P * (h - 1):P * h], n=T, tiles=2))
        for i in range(NT):
            job_gr = job("b_token", "act", [g_rp], tile=i, start=0, n=512, dest=g_raw[:, i, :], tanh=g_tanh[:, i, :])
        even_end = len(jobs)
        for h in range(4):
            job("ret_turn", "act", [], head=h, dest=yT[:, h, :], n=T)
        job_mix0 = mix_jobs("even_out")
        even_mix_end = len(jobs)
        turned_x(COL_LNG, COL_LNB)
        even_all_end = len(jobs)
        ffn_panels = [(panel("ffn"), panel("ffn"))]
        job_xt1 = turned_x(COL_LNG + 8, COL_LNB + 8)
        gp = panel("odd_in", 4096, 8)
        job_og = job("gates", "dve", [gp], after=job_xt1[2:])
        vp = [panel("odd_in", 2048 + 512 * n, 512) for n in range(2)]
        for half in range(2):
            for i in range(NT):
                job("b_token", "dve", [vp[half]], tile=i, start=0, n=512, dest=v_o[:, i, 512 * half:512 * half + 512])
                if (half, i) == (0, 1):
                    job_cum = job("cumsum", "dve", [])
                if (half, i) == (1, 0):
                    job_lt = job("low_turn", "act", [], after=[job_cum], dest=low_iT[0:4, :], n=T, rows=slice(0, 4))
        job_brow = [job("row_spread", "dve", [], head=h, after=[job_lt]) for h in range(4)]
        blocks = []

        def conv_blocks(c0):
            q = panel("odd_in", c0, 512)
            for m in range(4):
                yield lambda m=m: (blocks.append(c0 // P + m),
                                   job("conv", "dve", [q], start=P * m, block=c0 // P + m, order=len(blocks) - 1))

        for c0 in (0, 1024):
            for make in conv_blocks(c0):
                make()
        units_o = [(h, i) for h in range(4) for i in range(NT)]
        score_job, turn_job, value_job = {}, {}, {}
        mains = [m for c0 in (512, 1536) for m in conv_blocks(c0)]
        for s_ in range(len(units_o) + 2):
            if s_ < len(units_o):
                score_job[s_] = job("ml_scores", "dve", [], u=s_, convs=8 if s_ < 4 else 16)
            if s_ < 4:
                mains[2 * s_]()
            elif s_ < 8:
                if s_ % 2 == 0:
                    op = panel("odd_in", 3072 + 512 * (s_ // 2 - 2), 512)
                half = s_ // 2 - 2
                job_o_last = job("b_token", "act", [op], tile=s_ % 2, start=0, n=512, dest=None,
                    tanh=o_tanh[:, s_ % 2, 512 * half:512 * half + 512])
            if 1 <= s_ <= len(units_o):
                h, i = units_o[s_ - 1]
                turn_job[s_ - 1] = job("ml_turn", "act", [], u=s_ - 1, after=[score_job[s_ - 1]],
                                       dest=probT_sb[:, 512 * ((s_ - 1) % 2):512 * ((s_ - 1) % 2) + P * (i + 1)], n=P * (i + 1))
            if s_ < 4:
                mains[2 * s_ + 1]()
            if s_ >= 2:
                value_job[s_ - 2] = job("ml_value", "dve", [], u=s_ - 2, after=[turn_job[s_ - 2]])
        job_yt = [job("y_turn", ("act", "dve")[q % 2], [], quarter=q) for q in range(4)]
        job_mix1 = mix_jobs("odd_out")
        odd_mix_end = len(jobs)
        turned_x(COL_LNG + 16, COL_LNB + 16)
        ffn_panels.append((panel("ffn"), panel("ffn")))

        units = [("window", j, i) for j in range(4) for i in range(NT)]
        units += [("diff", j, i) for j in range(4) for i in range(NT)]
        units += [(kind, j, i) for j in range(4) for i in range(NT) for kind in ("select", "local")]
        n_units = len(units)
        units += [("dilated", j, i) for j in range(4) for i in range(NT)]
        group_of = [u if u < 16 else (16 + (u - 16) // 2 if u < n_units else u - 8) for u in range(len(units))]
        last_of_group = [u == len(units) - 1 or group_of[u + 1] != group_of[u] for u in range(len(units))]

        def spread(lo, hi, first, last):
            n, m = hi - lo, last - first
            return [range(lo + n * s // m, lo + n * (s + 1) // m) for s in range(m)]

        steps = spread(first_a, first_b, 0, 8) + spread(first_b, first_c, 8, 16)
        steps += spread(first_c, steps_end, 16, 32) + [range(0)] * 2
        steps_b = spread(first_even, even_end, n_units, len(units)) + [range(0)] * 2

        emptied, count = [], dict(act=0, dve=0)
        for jb in jobs:
            count[jb["engine"]] += 1
            emptied.append(count[jb["engine"]])
        last_job = {}
        for n, jb in enumerate(jobs):
            for q in jb["panels"]:
                last_job[q] = n
        slot_total, panel_full = [0] * 4, []
        for q, pl in enumerate(panels):
            slot_total[q % 4] += {"branch": 16 if pl[1:] == (1,) else 32, "ffn": 0}.get(pl[0], 16)
            panel_full.append(slot_total[q % 4])

        rows_in, const_in, x_in, modb_in = sem("rows_in"), sem("const_in"), sem("x_in"), sem("modb_in")
        bias_in, cmp_in_sem = sem("bias_in"), sem("cmp_weights_in")
        rows_turned, cols_ready = sem("rows_turned"), sem("cols_ready")
        silu_tanh, silu_ready = sem("silu_tanh"), sem("silu_ready")
        mod0_done, modrow_ready, mod_turned, mod_ready = sem("mod0_done"), sem("modrow_ready"), sem("mod_turned"), sem("mod_ready")
        std_ready, xn_ready = sem("std_ready"), sem("xn_ready")
        x_turned, hT_act, hT_dve = sem("x_turned"), sem("hT_act"), sem("hT_dve")
        slot_in = [sem(f"panel_slot{n}_in") for n in range(4)]
        job_done = sem("job_done")
        job_empty = dict(act=sem("job_emptied_by_act"), dve=sem("job_emptied_by_dve"))
        scores_done, max_done, exp_done = sem("scores_done"), sem("max_done"), sem("exp_done")
        norm_done, turned, turned_copied = sem("norm_done"), sem("prob_turned"), sem("probT_copied")
        pv_done, out_copied = sem("pv_done"), sem("out_copied")
        cmp_ready, gelu_in, gelu_tanh, hid_ready = sem("cmp_in_ready"), sem("gelu_in"), sem("gelu_tanh"), sem("hidden_ready")
        cmp_exp_in, cmp_exp, cmp_prob_ready = sem("cmp_exp_in"), sem("cmp_exp"), sem("cmp_prob_ready")
        diff_std, diff_ready = sem("diff_std"), sem("diff_normed")
        lam_sums, lam_exps = sem("lambda_sums"), sem("lambda_exps")
        act_own, dve_own = Tally(sem("act_own")), Tally(sem("dve_own"))
        nsa_tanh = sem("nsa_gates_tanh")
        cmp_half = sem("cmp_scores_half")
        router_in, std2_ready, xn2_ready = sem("router_in"), sem("std2_ready"), sem("xn2_ready")
        x2_turned, h2T_act, h2T_dve = sem("x2_turned"), sem("h2T_act"), sem("h2T_dve")
        logits_done, top_ready, top_exp, chosen_ready = sem("logits_done"), sem("top_ready"), sem("top_exp"), sem("chosen_ready")
        places_done, gatesT_ready, route_ready = sem("places_done"), sem("gatesT_ready"), sem("route_ready")
        w1_in = [sem(f"w1_chunk{k}_in") for k in range(KD)]
        w2_in = [sem(f"w2_chunk{k}_in") for k in range(KD)]
        b1_in = sem("expert_b1_in")
        w1_used, w2_used = sem("w1_chunks_used"), sem("w2_chunks_used")
        select_ready, gathered, info_done, spread_ready = sem("select_ready"), sem("gathered"), sem("slot_info_done"), sem("spread_ready")
        xg_lo, xg_hi = sem("gathered_low_copied"), sem("gathered_high_copied")
        gate_ready, tanh_ready, hidden_ready = sem("gate_part_ready"), sem("gate_tanh_ready"), sem("hidden_ready_moe")
        hidden_turned, hiddenT_ready, y_ready, spread_done = (
            sem("hidden_turned"), sem("hiddenT_ready"), sem("y_ready"), sem("spread_done"))
        ov = {n: sem("more_" + n) for n in ("select", "gathered", "xg", "hidden", "gate", "tanh", "act", "turned",
                                            "copied", "y", "y_copied", "done")}
        main_steps = {n: sem("dve_" + n) for n in ("clipped", "up_times_gate", "slot_data")}
        more_steps = {n: sem("dve_more_" + n) for n in ("clipped", "up_times_gate", "slot_data", "scaled")}
        moe_out_ready = sem("moe_out_ready")
        stored = sem("stored")
        bias_vectors_in, bias_row_done, bias_row_ready = sem("bias_vectors_in"), sem("bias_row_done"), sem("bias_row_ready")
        bias_stored, bias_in_b, consts_b_in, gate_b_in, final_in = (
            sem("bias_rows_stored"), sem("bias_tiles_in"), sem("consts_b_in"), sem("gate_b_in"), sem("final_vectors_in"))
        x2_std, z_ready, z_var, z_std, z_normed = sem("x2_std"), sem("z_ready"), sem("z_var"), sem("z_std"), sem("z_normed")
        ret_var, ret_std, ret_ready = sem("ret_var"), sem("ret_std"), sem("ret_ready")
        abs_ready, exp_abs_ready, log_f_ready, e_in, e_ready = (
            sem("gate_abs_ready"), sem("log_parts_ready"), sem("log_f_ready"), sem("exponents_ready"), sem("exps_ready"))
        conv_tanh, conv_done, y_odd_ready = sem("conv_tanh"), sem("conv_done"), sem("y_odd_ready")
        two = range(2)
        ffn_up_in, ffn_down_in = [sem(f"ffn_up_in{b}") for b in two], [sem(f"ffn_down_in{b}") for b in two]
        ffn_sums, ffn_step = [sem(f"ffn_sums{b}") for b in two], [sem(f"ffn_conv_step{b}") for b in two]
        ffn_conv, ffn_tanh = [sem(f"ffn_conv{b}") for b in two], [sem(f"ffn_tanh{b}") for b in two]
        ffn_act, ffn_used = [sem(f"ffn_act{b}") for b in two], [sem(f"ffn_used{b}") for b in two]
        tile_ready = sem("tile_ready")

        block = ctx.enter_context(nc.Block())

        def empty(eng, n):
            eng.wait_ge(job_empty[jobs[n]["engine"]], emptied[n])

        def col(n):
            return cols[:, n:n + 1]

        rows_dmas = []

        @block.sync
        def _(sp):
            sp.dma_start(x_res, a["x"].rearrange("b (i p) d -> p (b i) d", p=P)).then_inc(x_in, 16)
            for q, pl in enumerate(panels[:n_panels]):
                if q == q_b[0]:
                    sp.wait_ge(job_done, last_gate + 1)
                    sp.dma_start(exp_b2[0:N_EXP, :], a["exp_b2"][0]).then_inc(router_in, 16)
                    sp.dma_start(router_w, a["router_w"][0].rearrange("(k p) e -> p k e", p=P)).then_inc(router_in, 16)
                    sp.dma_start(router_b[0:1, :], a["router_b"]).then_inc(router_in, 16)
                if q >= 4:
                    if q - 4 < 4:
                        sp.wait_ge(mod0_done, q - 3)
                    else:
                        sp.wait_ge(job_done, last_job[q - 4] + 1)
                slot = ring[q % 4]
                arrived = slot_in[q % 4]
                if pl[0] == "mod":
                    _, g, c = pl
                    sp.dma_start(slot.rearrange("p (k n) -> p k n", k=2),
                                 a["mod_w"][0, 256 * c:256 * c + 256, 2048 * g:2048 * g + 2048]
                                 .rearrange("(k p) n -> p k n", p=P)).then_inc(arrived, 16)
                elif pl[0] == "in":
                    _, c0, n = pl
                    sp.dma_start(slot.rearrange("p (k n) -> p k n", k=KD)[:, :, 0:n],
                                 a["w_in"][0, :, c0:c0 + n].rearrange("(k p) n -> p k n", p=P)).then_inc(arrived, 16)
                elif pl[0] == "cmp":
                    sp.dma_start(slot.rearrange("p (k n) -> p k n", k=16),
                                 a["cmp_w1"][0, pl[1]].rearrange("(k p) n -> p k n", p=P)).then_inc(arrived, 16)
                elif pl[0] == "branch":
                    view = slot.rearrange("p (k n) -> p k n", k=4)
                    w = a["w_branch"][0, pl[1]]
                    if pl[1] == 1:
                        sp.dma_start(view, w.rearrange("(k p) n -> p k n", p=P)).then_inc(arrived, 16)
                    else:
                        for half in range(2):
                            sp.dma_start(view[64 * half:64 * half + 64],
                                         w[256 * half:256 * half + 256].rearrange("(k p) n -> p k n", p=64))\
                              .then_inc(arrived, 16)
                else:
                    sp.dma_start(slot.rearrange("p (k n) -> p k n", k=KD),
                                 a["w_out"][0, :, 512 * pl[1]:512 * pl[1] + 512]
                                 .rearrange("(k p) n -> p k n", p=P)).then_inc(arrived, 16)

            sp.wait_ge(job_done, n_jobs)
            sp.dma_start(cb, a["const_b"]).then_inc(consts_b_in, 16)
            sp.dma_start(rel_bias[0:32], a["rel_bias_2"]).then_inc(bias_vectors_in, 16)
            sp.dma_start(rel_onehot[0:32], a["onehot"]).then_inc(bias_vectors_in, 16)
            sp.dma_start(gate_b[0:1], a["odd_gate_b_2"]).then_inc(gate_b_in, 16)
            def expert_row(name, e, rows_):
                which = slice(e, e + 1) if isinstance(e, int) else bass.ds(e, 1)
                return a[name][0, which, rows_, :].rearrange("o p n -> (o p) n")

            def load_expert(e, wait_chunk, wait_output):
                which = slice(e, e + 1) if isinstance(e, int) else bass.ds(e, 1)
                for n, k in enumerate(W1_ORDER):
                    wait_chunk(n)
                    if n == 0:
                        sp.dma_start(exp_b1[0:P:32, :], a["exp_b1"][0, which, :].rearrange("o (r n) -> (o r) n", r=4))\
                          .then_inc(b1_in, 16)
                    sp.dma_start(w1[k], expert_row("exp_w1", e, slice(P * k, P * k + P))).then_inc(w1_in[k], 16)
                for k in range(KD):
                    wait_output(k)
                    sp.dma_start(w2[k], expert_row("exp_w2", e, slice(P * k, P * k + P))).then_inc(w2_in[k], 16)

            load_expert(0, lambda n: None, lambda k: None)
            def wait_used(count_, value):
                sp.wait_ge(count_, value)
                sp.nop(nofuse=True)

            with sp.Fori(1, N_EXP) as e:
                load_expert(e, lambda n: wait_used(w1_used, e * KD + (n + 1 - KD)),
                            lambda k: wait_used(w2_used, e * KD + (k + 1 - KD)))

            def load_panel(q):
                pl = panels[q]
                if q - n_panels < 4:
                    sp.wait_ge(w1_used, N_EXP * KD)
                elif panels[q - 4][0] == "ffn":
                    layer = int(q - 4 > ffn_panels[0][1])
                    b = ffn_panels[layer].index(q - 4)
                    sp.wait_ge(ffn_used[b], 11 * layer + 12)
                else:
                    sp.wait_ge(job_done, last_job[q - 4] + 1)
                if pl[0] == "ffn":
                    return
                name = pl[0][:4].rstrip("_")
                if pl[0].endswith("_out"):
                    c0, n, w = 512 * pl[1], 512, a[name + "_w_out_2"]
                else:
                    c0, n, w = pl[1], pl[2], a[name + "_w_in_2"]
                sp.dma_start(ring[q % 4].rearrange("p (k n) -> p k n", k=KD)[:, :, 0:n],
                             w[0, :, c0:c0 + n].rearrange("(k p) n -> p k n", p=P)).then_inc(slot_in[q % 4], 16)

            def load_ffn_up(layer, b, c):
                place = ring[ffn_panels[layer][b] % 4]
                w = a["ffn_w_up_2"][layer]
                for half in range(2):
                    columns_ = slice(D_FF * half + P * c, D_FF * half + P * c + P) if isinstance(c, int) else \
                        bass.ds(c * P + D_FF * half, P)
                    sp.dma_start(place[:, 1024 * half:1024 * half + 1024].rearrange("p (k n) -> p k n", k=KD),
                                 w[:, columns_].rearrange("(k p) n -> p k n", p=P)).then_inc(ffn_up_in[b], 16)

            def load_ffn_down(layer, b, c):
                rows_ = slice(P * c, P * c + P) if isinstance(c, int) else bass.ds(c * P, P)
                sp.dma_start(ring[ffn_panels[layer][b] % 4][:, 2048:3072],
                             a["ffn_w_down_2"][layer, rows_, :]).then_inc(ffn_down_in[b], 16)

            def ffn_weights(layer):
                with sp.Fori(1, NF // 2) as e:
                    for b in range(2):
                        wait_used(ffn_sums[b], e + 11 * layer)
                        load_ffn_up(layer, b, e * 2 + b)
                    for b in range(2):
                        wait_used(ffn_used[b], e + (11 * layer + 1))
                        load_ffn_down(layer, b, e * 2 + b)

            for q in range(n_panels, n_panels + 4):
                load_panel(q)
            sp.wait_ge(bias_row_ready, 1)
            sp.dma_start(scratch, bias_row[0:8, :].rearrange("p (o n) -> p o n", o=1).to_broadcast([8, P, 384]))\
              .then_inc(bias_stored, 16)
            sp.wait_ge(bias_stored, 16)
            sp.wait_ge(moe_out_ready, 1)
            for lo, n, base in ((0, P, T - 1), (P, T, P - 1)):
                skewed = bass.AP(tensor=scratch.tensor, offset=scratch.offset + base, ap=[[383, P], [384 * P, 8], [1, n]])
                sp.dma_start(toep[:, :, lo:lo + n], skewed).then_inc(bias_in_b, 16)
            for q in range(n_panels + 4, ffn_panels[0][0]):
                load_panel(q)
            for b in range(2):
                load_panel(ffn_panels[0][b])
                load_ffn_up(0, b, b)
                load_ffn_down(0, b, b)
            ahead = ffn_panels[0][1] + 1
            for q in range(ahead, ahead + 2):
                load_panel(q)
            ffn_weights(0)
            for q in range(ahead + 2, ffn_panels[1][0]):
                load_panel(q)
            sp.dma_start(final_gb[:, 0, :], a["ln_g_2"][1, 1:2, :].to_broadcast([P, D])).then_inc(final_in, 16)
            sp.dma_start(final_gb[:, 1, :], a["ln_b_2"][1, 1:2, :].to_broadcast([P, D])).then_inc(final_in, 16)
            for b in range(2):
                load_panel(ffn_panels[1][b])
                load_ffn_up(1, b, b)
                load_ffn_down(1, b, b)
            ffn_weights(1)
            for i in range(NT):
                sp.wait_ge(tile_ready, i + 1)
                sp.dma_start(out[0, P * i:P * i + P, :], z[:, i, :]).then_inc(stored, 16)
            sp.wait_ge(stored, 32)

        @block.scalar
        def _(act):
            own = act_own
            b_in = a["b_in"]

            def row_dma(row, n, src, sub=slice(0, P)):
                act.dma_start(rows[row:row + n, 0, sub], src).then_inc(rows_in, 16)
                rows_dmas.append(16)

            def flat(src, n):
                return src.rearrange("(k p) -> k p", p=n)

            act.dma_start(rows[ROW_C:ROW_C + 8, 0, :], flat(a["c"][0], P)).then_inc(rows_in, 16)
            rows_dmas.append(16)
            row_dma(ROW_N1, 8, flat(a["norm1_g"][0], P))
            row_dma(ROW_N2, 8, flat(a["norm2_g"][0], P))
            for at, base in ((A_Q0, BI_QA), (C_Q0, BI_QC)):
                for half in range(2):
                    row_dma(ROW_B + base, 4, flat(b_in[0, at + 256 * half:at + 256 * half + 256], 64),
                            slice(64 * half, 64 * half + 64))
            for at, base, n in ((A_K0, BI_KA, 1), (B_Q0, BI_QB, 4), (B_K0, BI_KB, 4), (C_KSEL0, BI_KSEL, 1),
                                (C_KWIN0, BI_KWIN, 1), (MERGE0, BI_GATE, 24)):
                row_dma(ROW_B + base, n, flat(b_in[0, at:at + 128 * n], P))
            for half in range(2):
                row_dma(ROW_B + BI_KCMP, 4, flat(b_in[0, C_KCMP0:C_KCMP0 + 256], 64), slice(64 * half, 64 * half + 64))
                row_dma(ROW_B2, 1, flat(a["cmp_b2"][0, 0], 64), slice(64 * half, 64 * half + 64))
            row_dma(ROW_SUB, 1, flat(a["diff_subln_g"][0], P))
            row_dma(ROW_FG, 8, flat(a["final_g"], P))
            row_dma(ROW_POS, 32, a["cmp_pos"][0].rearrange("n (m l) d -> (n m) (l d)", l=2))
            for layer in range(2):
                act.dma_start(rows[0:3 * NF, 1 + layer, :],
                              a["ffn_conv_w_2"][layer].rearrange("l (k p) -> (l k) p", p=P)).then_inc(rows_in, 16)
                act.dma_start(rows[3 * NF:4 * NF, 1 + layer, :],
                              flat(a["ffn_conv_b_2"][layer], P)).then_inc(rows_in, 16)
            act.dma_start(rows[0:N_ROWS_O, 3, :],
                          a["odd_conv_w_2"][0].rearrange("l (k p) -> (l k) p", p=P)).then_inc(rows_in, 16)
            for n, name in enumerate(("ln_g_2", "ln_b_2")):
                act.dma_start(rows[N_ROWS_O + 32 * n:N_ROWS_O + 32 * n + 32, 3, :],
                              a[name].rearrange("l s (k p) -> (l s k) p", p=P)).then_inc(rows_in, 16)
            rows_dmas.extend([16] * 7)
            act.dma_start(const, a["const_a"]).then_inc(const_in, 16)
            act.dma_start(start_const, a["const_s"]).then_inc(const_in, 16)
            act.dma_start(lam_row, a["diff_lambda"].rearrange("o a b -> o (a b)").to_broadcast([P, 256])).then_inc(const_in, 16)
            act.dma_start(sinks, a["sinks"].to_broadcast([P, 8])).then_inc(const_in, 16)
            for r in range(4):
                act.dma_start(modrow[32 * r:32 * r + 32],
                              a["mod_b"][0:1].rearrange("o (g r n) -> o g r n", g=3, r=4)[:, :, r, :]
                              .to_broadcast([32, 3, 512])).then_inc(modb_in, 16)
            at = 0
            for c0, n in ((A_V0, 128), (B_V0, 512), (C_VSEL0, 128), (C_VWIN0, 152)):
                act.dma_start(b_row[0:1, at:at + n], b_in[0:1, c0:c0 + n]).then_inc(bias_in, 16)
                at += n
            act.dma_start(cmp_b1[0:1, :], a["cmp_b1"].rearrange("o a b -> o (a b)")).then_inc(cmp_in_sem, 16)
            act.dma_start(cmp_b2v[0:1, :], a["cmp_b2"][0, 1:2]).then_inc(cmp_in_sem, 16)
            act.dma_start(cmp_w2, a["cmp_w2"][0].rearrange("n (k p) d -> p (n k) d", p=P)).then_inc(cmp_in_sem, 16)

            act.wait_ge(cols_ready, 1)
            act.activation(silu_c, cols[:, ROW_C:ROW_C + 8], ACT.Tanh, scale=0.5).then_inc(silu_tanh, 1)
            act.wait_ge(lam_sums, 1)
            act.activation(lam_sum[:, 2:4], lam_sum[:, 0:2], ACT.Exp).then_inc(lam_exps, 1)
            act.wait_ge(x_in, 16)
            for i in range(NT):
                ins = act.activation(xn[:, i, :], x_res[:, i, :], ACT.Square, accum_out=sumsq[:, i:i + 1])
            own.add(ins)
            act.wait_ge(own.sem, own.n)
            own.add(act.activation(sumsq, sumsq, ACT.Copy, scale=1.0 / D, bias=EPS))
            act.wait_ge(own.sem, own.n)
            act.activation(rstd, sumsq, ACT.Sqrt).then_inc(std_ready, 1)
            act.wait_ge(mod_ready, 1)
            for q in (0, 2):
                act.wait_ge(x_turned, q + 1)
                for k in (2 * q, 2 * q + 1):
                    act.activation(hT[:, k, :], bank[4 + q][:, T * (k % 2):T * (k % 2) + T], ACT.Identity,
                                   scale=scale1[:, k:k + 1], bias=mod[:, k:k + 1]).then_inc(hT_act, 1)

            def exps(u):
                kind, j, i = units[u]
                nk = P * (i + 1)
                act.wait_ge(max_done, u + 1)
                if u >= 2:
                    act.wait_ge(turned, u - 1)
                if kind == "window":
                    act.activation(unit_stat[:, 2, 2 * u:2 * u + 2], unit_stat[:, 2, 2 * u:2 * u + 2], ACT.Exp)
                for hh in range(2):
                    at = 512 * (u % 2) + 256 * hh
                    ins = act.activation(prob[:, at:at + nk], score_sb[:, at:at + nk], ACT.Exp,
                                         bias=unit_stat[:, 0, 2 * u + hh:2 * u + hh + 1],
                                         accum_out=unit_stat[:, 1, 2 * u + hh:2 * u + hh + 1])
                ins.then_inc(exp_done, 1)

            def copy_turned(u):
                kind, j, i = units[u]
                n = P * (i + 1) * (1 if kind == "diff" else 2)
                act.wait_ge(turned, u + 1)
                if u >= 2:
                    act.wait_ge(pv_done, u - 1)
                act.activation(probT_sb[:, 512 * (u % 2):512 * (u % 2) + n], bank[4 + u % 2][:, 0:n],
                               ACT.Copy).then_inc(turned_copied, 1)

            def copy_out(u):
                if not last_of_group[u]:
                    return
                kind, j, i = units[u]
                g = group_of[u]
                act.wait_ge(pv_done, u + 1)
                if kind == "diff":
                    dest = o_tok[:, i, P * j:P * j + P]
                elif kind == "dilated":
                    dest = yT[:, 4 + j, P * i:P * i + P]
                else:
                    dest = oT[0 if kind == "window" else 2][:, j, P * i:P * i + P]
                act.activation(dest, bank[6 + g % 2][:, 0:P], ACT.Copy).then_inc(out_copied, 1)

            def empty_job(n):
                jb = jobs[n]
                if jb["kind"] == "gates":
                    act.wait_ge(abs_ready, 1)
                    own.add(act.activation(log_f, log_f, ACT.Exp, scale=-1.0))
                    act.wait_ge(own.sem, own.n)
                    act.activation(log_f, log_f, ACT.Ln, bias=ones[:, 0:1]).then_inc(exp_abs_ready, 1)
                if jb["kind"] == "row_spread" and jb["head"] == 3:
                    act.wait_ge(e_in, 1)
                    for h in range(4):
                        for i, part in enumerate((slice(0, P), slice(P, 3 * P))):
                            act.activation(expD[:, h, part], expD[:, h, part], ACT.Exp, bias=neg_r[:, i, h:h + 1])
                    act.activation(floor_e, floor_e, ACT.Exp).then_inc(e_ready, 1)
                if jb["kind"] == "conv":
                    o_ = jb["order"]
                    empty(act, n)
                    act.activation(conv_t[:, o_ % 2, :], conv_acc[:, o_ % 2, :], ACT.Tanh, scale=0.5).then_inc(conv_tanh, 1)
                if jb["engine"] != "act":
                    return
                act.wait_ge(job_done, n + 1)
                src, kind = bank[n % 2], jb["kind"]
                if kind == "feature":
                    ins = act.activation(jb["dest"], src[:, 0:T], ACT.Identity, bias=col(ROW_B + jb["bias"]))
                elif kind == "shifted":
                    if n == job_shift0:
                        act.wait_ge(x_turned, 4)
                    act.activation(jb["dest"][0:64], src[0:64, 0:T], ACT.Identity, bias=col(ROW_B + jb["bias"])[0:64])
                    ins = act.activation(jb["dest"][64:128, 0:T - 1], src[64:128, 1:T], ACT.Identity,
                                         bias=col(ROW_B + jb["bias"])[64:128])
                elif kind == "cmp_hidden_t":
                    ins = act.activation(hidT.rearrange("p a b -> p (a b)"), src[:, 0:128], ACT.Copy)
                elif kind == "cmp_k":
                    ins = act.activation(kcT[:, 0:15], src[:, 0:15], ACT.Identity, bias=col(ROW_B2))
                elif kind == "cmp_v":
                    ins = act.activation(vcT[0:15].rearrange("p a b -> p (a b)"), src[0:15, 0:128], ACT.Copy)
                elif kind == "cmp_prob_t":
                    ins = act.activation(probT_cmp, src[:, 0:T], ACT.Copy)
                elif kind == "gate":
                    if jb["dest"] is jobs[first_c]["dest"]:
                        act.wait_ge(max_done, 8)
                    ins = act.activation(jb["dest"], src[:, 0:T], ACT.Tanh, scale=0.5, bias=col(ROW_B + jb["bias"]))
                elif kind == "broadcast":
                    if n == job_g1:
                        act.wait_ge(scores_done, n_units)
                    ins = act.activation(jb["dest"], src[:, :], ACT.Copy, scale=jb["factor"])
                elif kind == "diff_out_t":
                    ins = act.activation(oT[1][:, jb["head"], :], src[:, 0:T], ACT.Copy, scale=col(ROW_SUB))
                elif kind == "xt" or kind == "y_turn":
                    for k in (2 * jb["quarter"], 2 * jb["quarter"] + 1):
                        dest = (xT if kind == "xt" else yT)[:, k, :]
                        part = src[:, T * (k % 2):T * (k % 2) + T]
                        if kind == "y_turn":
                            ins = act.activation(dest, part, ACT.Copy, scale=0.5)
                        elif jb["b"] is None:
                            ins = act.activation(dest, part, ACT.Copy, scale=col(jb["g"] + k))
                        else:
                            ins = act.activation(dest, part, ACT.Identity, scale=col(jb["g"] + k), bias=col(jb["b"] + k))
                elif kind in ("b_feature", "ret_value", "ret_turn", "low_turn", "ml_turn", "mix_out_b", "b_token"):
                    n_ = jb.get("n", T)
                    rows_ = jb.get("rows", slice(0, P))
                    part = src[rows_, 0:n_]
                    if jb.get("tiles"):
                        part = part.rearrange("p (i n) -> p i n", i=2)
                    if jb["dest"] is not None:
                        ins = act.activation(jb["dest"], part, ACT.Copy)
                    if jb.get("tanh") is not None:
                        ins = act.activation(jb["tanh"], part, ACT.Tanh, scale=0.5)
                ins.then_inc(job_empty["act"], 1)

            job_shift0 = next(n for n, jb in enumerate(jobs) if jb["kind"] == "shifted")
            for n in range(first_a):
                empty_job(n)
            for s in range(n_units + 2):
                if s < n_units:
                    exps(s)
                for n in steps[s]:
                    if jobs[n]["kind"] == "cmp_hidden":
                        empty(act, job_gates)
                        flat_g = nsa_g.rearrange("p a b -> p (a b)")
                        act.activation(flat_g, flat_g, ACT.Tanh, scale=0.5).then_inc(nsa_tanh, 1)
                        act.wait_ge(gelu_in, 1)
                        act.activation(hid_t[0:64, :], hid_t[0:64, :], ACT.Tanh,
                                       scale=math.sqrt(2 / math.pi)).then_inc(gelu_tanh, 1)
                    if jobs[n]["kind"] == "cmp_scores":
                        act.wait_ge(cmp_exp_in, 1)
                        act.activation(cmp_s, cmp_s, ACT.Exp).then_inc(cmp_exp, 1)
                    empty_job(n)
                if 1 <= s <= n_units:
                    copy_turned(s - 1)
                if s >= 2:
                    copy_out(s - 2)
            act.wait_ge(out_copied, group_of[n_units - 1] + 1)
            for h in range(4):
                for i in range(NT):
                    ins = act.activation(score_sb[:, P * (4 * i + h):P * (4 * i + h) + P], o_tok[:, i, P * h:P * h + P], ACT.Square,
                                         accum_out=sub_stat[:, 4 * i + h:4 * i + h + 1])
            own.add(ins)
            act.wait_ge(own.sem, own.n)
            own.add(act.activation(sub_stat, sub_stat, ACT.Copy, scale=1.0 / P, bias=EPS))
            act.wait_ge(own.sem, own.n)
            act.activation(sub_stat, sub_stat, ACT.Sqrt).then_inc(diff_std, 1)
            for n in range(steps_end, n_jobs):
                empty_job(n)

            empty(act, n_jobs - 1)
            for i in range(NT):
                ins = act.activation(xn2[:, i, :], x_res[:, i, :], ACT.Square, accum_out=sumsq[:, i:i + 1])
            own.add(ins)
            act.wait_ge(own.sem, own.n)
            own.add(act.activation(sumsq, sumsq, ACT.Copy, scale=1.0 / D, bias=EPS))
            act.wait_ge(own.sem, own.n)
            act.activation(rstd, sumsq, ACT.Sqrt).then_inc(std2_ready, 1)
            act.wait_ge(xn2_ready, 1)
            for q in (0, 2):
                act.wait_ge(x2_turned, q + 1)
                for k in (2 * q, 2 * q + 1):
                    act.activation(h2T[:, k, :], bank[2 + q][:, T * (k % 2):T * (k % 2) + T], ACT.Identity,
                                   scale=scale2[:, k:k + 1], bias=mod[:, 24 + k:25 + k]).then_inc(h2T_act, 1)
            act.wait_ge(top_ready, 1)
            for i in range(NT):
                ins = act.activation(top_gate[:, i, :], best[:, i, 0:TOP_K], ACT.Exp, bias=top_stat[:, i:i + 1],
                                     accum_out=top_stat[:, 2 + i:3 + i])
            ins.then_inc(top_exp, 1)

            def copy_gathered(n):
                act.wait_ge(gathered, n)
                for k in range(4):
                    ins = act.activation(xgT[:, k, :], bank[7][:, P * k:P * k + P], ACT.Identity,
                                         scale=scale2[:, k:k + 1], bias=mod[:, 24 + k:25 + k])
                ins.then_inc(xg_lo, 1)

            def gate_and_turn(gate_sem, tanh_sem, turned_sem, copied_sem, n, between=None):
                act.wait_ge(gate_sem, n)
                act.activation(gate_tanh, gate_part, ACT.Tanh, scale=0.5 * 1.702).then_inc(tanh_sem, 1)
                if between:
                    between()
                act.wait_ge(turned_sem, n)
                act.activation(hiddenT.rearrange("p a b -> p (a b)"), bank[7], ACT.Copy, scale=0.5).then_inc(copied_sem, 1)

            copy_gathered(1)
            with act.Fori(0, N_EXP) as e:
                count = act.value_load(counts_int_i[0:1, bass.ds(e, 1)], min_val=0, max_val=T)
                before = act.value_load(before_int_i[0:1, bass.ds(e, 1)], min_val=0, max_val=3 * N_EXP)
                def further_pass(p):
                    n = before + p
                    gate_and_turn(ov["gate"], ov["tanh"], ov["turned"], ov["copied"], n)
                    act.wait_ge(ov["y"], n)
                    act.activation(y_ov, bank[6], ACT.Copy).then_inc(ov["y_copied"], 1)
                    act.wait_ge(ov["done"], n)
                    act.nop(nofuse=True)

                with act.If(count > SLOTS):
                    further_pass(1)
                    with act.If(count > 2 * SLOTS):
                        further_pass(2)
                        with act.If(count > 3 * SLOTS):
                            further_pass(3)
                gate_and_turn(gate_ready, tanh_ready, hidden_turned, hiddenT_ready, e + 1, lambda: copy_gathered(e + 2))
                act.wait_ge(w2_used, e * KD + KD)
                act.activation(y_sb, bank[6], ACT.Copy).then_inc(y_ready, 1)

            act.wait_ge(moe_out_ready, 1)
            for i in range(NT):
                ins = act.activation(z[:, i, :], x_res[:, i, :], ACT.Square, accum_out=sumsq[:, i:i + 1])
            own.add(ins)
            act.wait_ge(own.sem, own.n)
            own.add(act.activation(sumsq, sumsq, ACT.Copy, scale=1.0 / D, bias=EPS))
            act.wait_ge(own.sem, own.n)
            act.activation(rstd, sumsq, ACT.Sqrt).then_inc(x2_std, 1)
            for n in range(n_jobs, first_even):
                empty_job(n)
            for s in range(n_units, len(units) + 2):
                if s < len(units):
                    exps(s)
                for n in steps_b[s - n_units]:
                    empty_job(n)
                if n_units < s <= len(units):
                    copy_turned(s - 1)
                if s >= n_units + 2:
                    copy_out(s - 2)
            act.wait_ge(ret_var, 1)
            act.activation(ret_mv[:, :, 1], ret_mv[:, :, 1], ACT.Sqrt).then_inc(ret_std, 1)
            for n in range(even_end, even_mix_end):
                empty_job(n)

            def layer_norm_roots(n):
                for i in range(NT):
                    act.wait_ge(z_var, 2 * n + i + 1)
                    act.activation(ln_mv[:, i, 1:2], ln_mv[:, i, 1:2], ACT.Sqrt).then_inc(z_std, 1)

            def ffn_gates(layer):
                with act.Fori(0, NF // 2) as e:
                    for b in range(2):
                        act.wait_ge(ffn_conv[b], e + 11 * layer + 1)
                        act.activation(ffn_t[:, b, :], ffn_z[:, b, :], ACT.Tanh, scale=0.5).then_inc(ffn_tanh[b], 1)
                act.wait_ge(ffn_used[1], 11 * layer + 12)
                for i in range(NT):
                    for half in range(2):
                        ins = act.activation(z[:, i, 512 * half:512 * half + 512], bank[2 * i + half], ACT.Copy)
                    ins.then_inc(z_ready, 1)

            layer_norm_roots(0)
            for n in range(even_mix_end, even_all_end):
                empty_job(n)
            ffn_gates(0)
            layer_norm_roots(1)
            for n in range(even_all_end, odd_mix_end):
                empty_job(n)
            layer_norm_roots(2)
            for n in range(odd_mix_end, len(jobs)):
                empty_job(n)
            ffn_gates(1)
            layer_norm_roots(3)

        @block.tensor
        def _(pe):
            pe.wait_ge(rows_in, sum(rows_dmas))
            pe.wait_ge(const_in, 64)
            at = 0
            for n, (table, count_) in enumerate(((0, N_ROWS), (1, N_FROWS), (2, N_FROWS), (3, N_ROWS_O + 64))):
                ins = pe.transpose(bank[2][:, at:at + count_], rows[0:count_, table, :], ident[0:count_, 0:count_])
                at += count_
            ins.then_inc(rows_turned, 1)

            def mod_rows(target, q, c):
                pe.wait_ge(slot_in[q % 4], panel_full[q])
                w = ring[q % 4].rearrange("p (k n) -> p k n", k=2)
                for kk in range(2):
                    for r in range(4):
                        ins = pe.matmul(target[32 * r:32 * r + 32, :], silu32[:, 2 * c + kk, :],
                                        w[:, kk, 512 * r:512 * r + 512], start=(c == 0 and kk == 0),
                                        stop=(c == 3 and kk == 1), tile_position=(0, 32 * r))
                return ins

            def turn_mod(target, g):
                for j in range(4):
                    ins = pe.transpose(target[:, P * j:P * j + P], modrow[:, g, P * j:P * j + P], ident)
                return ins

            pe.wait_ge(silu_ready, 1)
            for c in range(4):
                mod_rows(bank[3], mod0[c], c).then_inc(mod0_done, 1)
            pe.wait_ge(modrow_ready, 1)
            turn_mod(bank[3], 0).then_inc(mod_turned, 1)
            pe.wait_ge(xn_ready, 1)
            for q in range(4):
                for kk in range(2):
                    for i in range(NT):
                        ins = pe.transpose(bank[4 + q][:, T * kk + P * i:T * kk + P * i + P],
                                           xn[:, i, P * (2 * q + kk):P * (2 * q + kk) + P], ident)
                ins.then_inc(x_turned, 1)
            pe.wait_ge(bias_in, 64)
            pe.wait_ge(hT_act, 4)
            pe.wait_ge(hT_dve, 4)

            def run_job(n):
                jb = jobs[n]
                kind, o = jb["kind"], bank[n % 2]
                if n >= 2:
                    empty(pe, n - 2)
                for q in jb["panels"]:
                    if kind != "mod":
                        pe.wait_ge(slot_in[q % 4], panel_full[q])
                for m in jb.get("after", ()):
                    empty(pe, m)
                if kind in ("feature", "shifted", "gate"):
                    w = ring[jb["panels"][0] % 4].rearrange("p (k n) -> p k n", k=KD)
                    for k in range(KD):
                        for half, start in enumerate(jb["starts"]):
                            m = P // len(jb["starts"])
                            ins = pe.matmul(o[m * half:m * half + m, 0:T], w[:, k, start:start + m], hT[:, k, :],
                                            start=(k == 0), stop=(k == KD - 1), tile_position=(0, m * half))
                elif kind == "token":
                    w = ring[jb["panels"][0] % 4].rearrange("p (k n) -> p k n", k=KD)
                    at, m = jb["start"], jb["n"]
                    pe.matmul(o[:, 0:m], ones[0:1, :], b_row[0:1, jb["row"]:jb["row"] + m], start=True, stop=False)
                    for k in range(KD):
                        ins = pe.matmul(o[:, 0:m], hT[:, k, P * jb["tile"]:P * jb["tile"] + P], w[:, k, at:at + m],
                                        start=False, stop=(k == KD - 1))
                elif kind == "cmp_hidden":
                    pe.wait_ge(cmp_in_sem, 48)
                    pe.wait_ge(cmp_ready, 1)
                    for kv in range(2):
                        w = ring[jb["panels"][kv] % 4].rearrange("p (k n) -> p k n", k=16)
                        rows_ = slice(32 * kv, 32 * kv + 32)
                        pe.matmul(o[rows_, 0:256], ones[0:1, 0:32], cmp_b1[0:1, 256 * kv:256 * kv + 256],
                                  start=True, stop=False, tile_position=(0, 32 * kv))
                        for m in range(16):
                            ins = pe.matmul(o[rows_, 0:256], cmp_in[:, kv, m, :], w[:, m, :], start=False,
                                            stop=(m == 15), tile_position=(0, 32 * kv))
                elif kind == "cmp_hidden_t":
                    pe.wait_ge(hid_ready, 1)
                    for c in range(2):
                        ins = pe.transpose(o[:, 64 * c:64 * c + 64], hid[0:64, P * c:P * c + P], ident[0:64, 0:64])
                elif kind == "cmp_k":
                    empty(pe, n - 1)
                    for c in range(2):
                        for g in range(2):
                            ins = pe.matmul(o[64 * g:64 * g + 64, 0:15], cmp_w2[:, c, :],
                                            hidT[:, c, 15 * g:15 * g + 15], start=(c == 0), stop=(c == 1),
                                            tile_position=(0, 64 * g))
                elif kind == "cmp_v":
                    for g in range(2):
                        pe.matmul(o[0:15, 64 * g:64 * g + 64], ones[0:1, 0:15], cmp_b2v[0:1, :], start=True, stop=False)
                        for c in range(2):
                            ins = pe.matmul(o[0:15, 64 * g:64 * g + 64], hidT[:, c, 32 + 15 * g:32 + 15 * g + 15],
                                            cmp_w2[:, 2 + c, :], start=False, stop=(c == 1))
                elif kind == "cmp_v_rep":
                    empty(pe, n - 1)
                    for g in range(2):
                        ins = pe.matmul(o[:, 0:64], cmp_rep[0:15, g, :], vcT[0:15, g, :], start=(g == 0), stop=(g == 1))
                elif kind == "cmp_scores":
                    empty(pe, job_cmp_qk - 3)
                    for g in range(2):
                        if g == 1:
                            pe.wait_ge(cmp_half, 1)
                        for i in range(NT):
                            for j in range(4):
                                at = P * i + 16 * (j + 4 * g)
                                ins = pe.matmul(o[:, at:at + 16], qcT[64 * g:64 * g + 64, j, P * i:P * i + P],
                                                kcT[64 * g:64 * g + 64, :], start=True, stop=True)
                        if g == 0:
                            ins.then_inc(cmp_half, 1)
                elif kind == "cmp_prob_t":
                    pe.wait_ge(cmp_prob_ready, 1)
                    for i in range(NT):
                        ins = pe.transpose(o[:, P * i:P * i + P], cmp_s[:, P * i:P * i + P], ident)
                elif kind == "mod":
                    for c, q in enumerate(jb["panels"]):
                        ins = mod_rows(o, q, c)
                elif kind == "mod_t":
                    empty(pe, n - 1)
                    ins = turn_mod(o, jb["group"])
                elif kind == "broadcast":
                    r = jb["row"]
                    ins = pe.matmul(o[:, :], ones[32 * r:32 * r + 1, :], modrow[32 * r:32 * r + 1, jb["group"], :],
                                    start=True, stop=True)
                elif kind == "diff_out_t":
                    pe.wait_ge(diff_ready, 1)
                    for i in range(NT):
                        ins = pe.transpose(o[:, P * i:P * i + P], o_tok[:, i, P * jb["head"]:P * jb["head"] + P], ident)
                elif kind == "branch":
                    k, br = jb["chunk"], jb["branch"]
                    if k == 0:
                        pe.wait_ge(slot_in[q_b[br] % 4], panel_full[q_b[br]])
                        pe.wait_ge(out_copied, group_of[n_units - 1] + 1)
                        empty(pe, job_ob[-1])
                    w = ring[q_b[br] % 4].rearrange("p (k n) -> p k n", k=4)
                    for f in range(4):
                        ins = pe.matmul(o[:, 0:T], w[:, f, P * k:P * k + P], oT[br][:, f, :],
                                        start=(f == 0), stop=(f == 3))
                elif kind == "mix_out":
                    empty(pe, n_jobs - 5)
                    w = ring[jb["panels"][0] % 4].rearrange("p (k n) -> p k n", k=KD)
                    for k in range(KD):
                        ins = pe.matmul(o[:, :], mergedT[:, k, P * jb["tile"]:P * jb["tile"] + P], w[:, k, :],
                                        start=(k == 0), stop=(k == KD - 1))
                elif kind == "xt":
                    if jb["quarter"] == 0:
                        pe.wait_ge(z_normed, 2 * xt_group[n] + 2)
                    for kk in range(2):
                        for i in range(NT):
                            k = 2 * jb["quarter"] + kk
                            ins = pe.transpose(o[:, T * kk + P * i:T * kk + P * i + P], z[:, i, P * k:P * k + P], ident)
                elif kind in ("b_feature", "conv"):
                    w = ring[jb["panels"][0] % 4].rearrange("p (k n) -> p k n", k=KD)
                    for k in range(KD):
                        ins = pe.matmul(o[:, 0:T], w[:, k, jb["start"]:jb["start"] + P], xT[:, k, :],
                                        start=(k == 0), stop=(k == KD - 1))
                elif kind == "b_token":
                    w = ring[jb["panels"][0] % 4].rearrange("p (k n) -> p k n", k=KD)
                    for k in range(KD):
                        ins = pe.matmul(o[:, :], xT[:, k, P * jb["tile"]:P * jb["tile"] + P], w[:, k, :],
                                        start=(k == 0), stop=(k == KD - 1))
                elif kind == "swap":
                    pe.wait_ge(consts_b_in, 16)
                    ins = pe.matmul(o[:, 0:T], cbc("swap"), raw[:, jb["m"], :], start=True, stop=True)
                elif kind == "ret_scores":
                    h = jb["head"]
                    pe.matmul(o[:, 0:T], rot[:, 4 + h, 0:P], rot[:, h, :], start=True, stop=True)
                    ins = pe.matmul(o[:, T:T + P], rot[:, 4 + h, P:T], rot[:, h, P:T], start=True, stop=True)
                elif kind == "ret_value":
                    h = jb["head"]
                    v = v_r[:, :, P * h:P * h + P]
                    pe.matmul(o[:, 0:P], decayed[:, h, 0:P], v[:, 0], start=True, stop=True)
                    pe.matmul(o[:, P:T], decayed[:, h, P:T], v[:, 0], start=True, stop=False)
                    ins = pe.matmul(o[:, P:T], decayed[:, h, T:T + P], v[:, 1], start=False, stop=True)
                elif kind == "ret_turn":
                    pe.wait_ge(ret_ready, 1)
                    for i in range(NT):
                        ins = pe.transpose(o[:, P * i:P * i + P], y_even[:, i, P * jb["head"]:P * jb["head"] + P], ident)
                elif kind == "mix_out_b":
                    if n == job_mix0:
                        pe.wait_ge(out_copied, group_of[-1] + 1)
                    w = ring[jb["panels"][0] % 4].rearrange("p (k n) -> p k n", k=KD)
                    residual(o, jb["tile"], jb["half"])
                    for k in range(KD):
                        ins = pe.matmul(o[:, :], yT[:, k, P * jb["tile"]:P * jb["tile"] + P], w[:, k, :],
                                        start=False, stop=True, skip_group_check=True)
                elif kind == "gates":
                    pe.wait_ge(gate_b_in, 16)
                    w = ring[jb["panels"][0] % 4].rearrange("p (k n) -> p k n", k=KD)
                    for i in range(NT):
                        pe.matmul(o[:, 8 * i:8 * i + 8], ones[0:1, :], gate_b[0:1, :], start=True, stop=False)
                        for k in range(KD):
                            ins = pe.matmul(o[:, 8 * i:8 * i + 8], xT[:, k, P * i:P * i + P], w[:, k, 0:8],
                                            start=False, stop=(k == KD - 1))
                elif kind == "cumsum":
                    pe.wait_ge(log_f_ready, 1)
                    pe.matmul(o[:, 0:4], ca("tri_incl"), log_f[:, 0, :], start=True, stop=True)
                    pe.matmul(o[:, 4:8], ones, log_f[:, 0, :], start=True, stop=False)
                    ins = pe.matmul(o[:, 4:8], ca("tri_incl"), log_f[:, 1, :], start=False, stop=True)
                elif kind == "low_turn":
                    for i in range(NT):
                        ins = pe.transpose(o[0:4, P * i:P * i + P], low_i[:, i, :], ident)
                elif kind == "row_spread":
                    ins = pe.matmul(o[:, 0:T], cbc("head_sel")[0:4, P * jb["head"]:P * jb["head"] + P], low_iT[0:4, :],
                                    start=True, stop=True)
                elif kind == "ml_scores":
                    pe.wait_ge(conv_done, jb["convs"])
                    h, i = units_o[jb["u"]]
                    for c in range(2):
                        ins = pe.matmul(o[:, 0:P * (i + 1)], qkT[:, 2 * h + c, P * i:P * i + P],
                                        qkT[:, KD + 2 * h + c, 0:P * (i + 1)], start=(c == 0), stop=(c == 1))
                elif kind == "ml_turn":
                    h, i = units_o[jb["u"]]
                    for kt in range(i + 1):
                        at = 512 * (jb["u"] % 2) + P * kt
                        ins = pe.transpose(o[:, P * kt:P * kt + P], prob[:, at:at + P], ident)
                elif kind == "ml_value":
                    h, i = units_o[jb["u"]]
                    for kt in range(i + 1):
                        at = 512 * (jb["u"] % 2) + P * kt
                        ins = pe.matmul(o[:, 0:T], probT_sb[:, at:at + P], v_o[:, kt, T * h:T * h + T],
                                        start=(kt == 0), stop=(kt == i))
                elif kind == "y_turn":
                    if jb["quarter"] == 0:
                        pe.wait_ge(y_odd_ready, 2)
                    for kk in range(2):
                        for i in range(NT):
                            k = 2 * jb["quarter"] + kk
                            ins = pe.transpose(o[:, T * kk + P * i:T * kk + P * i + P], y_odd[:, i, P * k:P * k + P], ident)
                ins.then_inc(job_done, 1)

            def residual(o, i, half):
                for c in range(4):
                    pe.matmul(o[:, P * c:P * c + P], xT[:, 4 * half + c, P * i:P * i + P], alpha_ident,
                              start=(c == 0), stop=True, skip_group_check=True)

            xt_group = {n: g for g, first in enumerate((n_jobs, even_mix_end, even_all_end, odd_mix_end))
                        for n in range(first, first + 4)}

            def scores(u):
                kind, j, i = units[u]
                if u >= 1:
                    pe.wait_ge(max_done, u)
                if u == 0:
                    empty(pe, first_a - 1)
                if u == 8:
                    empty(pe, first_b - 1)
                if u == 16:
                    empty(pe, first_c - 1)
                if u == n_units:
                    empty(pe, first_even - 3)
                    empty(pe, first_even - 1)
                q, k = {"window": (qaT, kaT), "diff": (qbT, None), "select": (qcT, kselT), "local": (qcT, kwinT),
                        "dilated": (qdT, None)}[kind]
                nk = P * (i + 1)
                for hh in range(2):
                    half = slice(64 * hh, 64 * hh + 64)
                    keys = (kdT if kind == "dilated" else kbT)[half, j, 0:nk] if k is None else k[half, 0:nk]
                    ins = pe.matmul(score_banks[:, hh, 0:nk], q[half, j, P * i:P * i + P], keys,
                                    start=True, stop=True)
                ins.then_inc(scores_done, 1)

            def turn(u):
                kind, j, i = units[u]
                pe.wait_ge(norm_done, u + 1)
                if u >= 2:
                    pe.wait_ge(turned_copied, u - 1)
                at = 0
                for hh in range(1 if kind == "diff" else 2):
                    for kt in range(i + 1):
                        src = 512 * (u % 2) + 256 * hh + P * kt
                        ins = pe.transpose(bank[4 + u % 2][:, at:at + P], prob[:, src:src + P], ident)
                        at += P
                ins.then_inc(turned, 1)

            def value(u):
                kind, j, i = units[u]
                g = group_of[u]
                first = u == 0 or group_of[u - 1] != g
                pe.wait_ge(turned_copied, u + 1)
                if g >= 2 and first:
                    pe.wait_ge(out_copied, g - 1)
                o, pt = bank[6 + g % 2], 512 * (u % 2)
                if kind == "diff":
                    for kt in range(i + 1):
                        ins = pe.matmul(o[:, 0:P], probT_sb[:, pt + P * kt:pt + P * kt + P],
                                        vtok[:, kt, 128 + P * j:128 + P * j + P], start=(kt == 0), stop=(kt == i))
                else:
                    v, v0 = {"window": (vtok, 0), "select": (vtok, 640), "local": (vtok, 768), "dilated": (v_d, P * j)}[kind]
                    alone = kind in ("window", "dilated")
                    for kt in range(i + 1):
                        for hh in range(2):
                            at = pt + P * ((i + 1) * hh + kt)
                            ins = pe.matmul(o[64 * hh:64 * hh + 64, 0:P], v[:, kt, v0 + 64 * hh:v0 + 64 * hh + 64],
                                            probT_sb[:, at:at + P], start=(first and kt == 0),
                                            stop=(alone and kt == i), tile_position=(0, 64 * hh))
                    if kind == "local":
                        if g == 16:
                            empty(pe, job_cmp_t)
                            empty(pe, job_cmp_t - 2)
                        for hh in range(2):
                            ins = pe.matmul(o[64 * hh:64 * hh + 64, 0:P], vz[:, j + 4 * hh, :],
                                            probT_cmp[:, P * i:P * i + P], start=False, stop=True,
                                            tile_position=(0, 64 * hh))
                ins.then_inc(pv_done, 1)

            for n in range(first_a):
                run_job(n)
            for s in range(n_units + 2):
                if s < n_units:
                    scores(s)
                for n in steps[s]:
                    run_job(n)
                if 1 <= s <= n_units:
                    turn(s - 1)
                if s >= 2:
                    value(s - 2)
            for n in range(steps_end, n_jobs):
                run_job(n)

            pe.wait_ge(xn2_ready, 1)
            for q in range(4):
                for kk in range(2):
                    for i in range(NT):
                        ins = pe.transpose(bank[2 + q][:, T * kk + P * i:T * kk + P * i + P],
                                           xn2[:, i, P * (2 * q + kk):P * (2 * q + kk) + P], ident)
                ins.then_inc(x2_turned, 1)
            pe.wait_ge(bias_vectors_in, 32)
            pe.matmul(bank[1][0:8, 0:384], rel_bias[0:32, :], rel_onehot[0:32, :], start=True, stop=True)\
              .then_inc(bias_row_done, 1)
            pe.wait_ge(router_in, 48)
            pe.wait_ge(h2T_act, 4)
            pe.wait_ge(h2T_dve, 4)
            for i in range(NT):
                pe.matmul(bank[6][:, 32 * i:32 * i + 32], ones[0:1, :], router_b[0:1, :], start=True, stop=False)
                for k in range(KD):
                    ins = pe.matmul(bank[6][:, 32 * i:32 * i + 32], h2T[:, k, P * i:P * i + P], router_w[:, k, :],
                                    start=False, stop=(k == KD - 1))
            ins.then_inc(logits_done, 1)
            pe.wait_ge(chosen_ready, 1)
            pe.matmul(bank[7][:, 0:32], ca("tri"), chosen[:, 0, :], start=True, stop=True)
            pe.matmul(bank[7][:, 32:64], ones, chosen[:, 0, :], start=True, stop=False)
            pe.matmul(bank[7][:, 32:64], ca("tri"), chosen[:, 1, :], start=False, stop=True)
            pe.matmul(bank[7][:, 64:96], ones, chosen[:, 0, :], start=True, stop=False)
            pe.matmul(bank[7][:, 64:96], ones, chosen[:, 1, :], start=False, stop=True)
            for i in range(NT):
                ins = pe.transpose(bank[7][0:N_EXP, P + P * i:2 * P + P * i], gates_t[:, i, :], ident)
            ins.then_inc(places_done, 1)
            pe.wait_ge(gatesT_ready, 1)
            for i in range(NT):
                for half in range(2):
                    pe.matmul(bank[2 * i + half], gatesT[0:N_EXP, P * i:P * i + P],
                              exp_b2[0:N_EXP, 512 * half:512 * half + 512], start=True, stop=True)

            def gather(n):
                pe.wait_ge(select_ready, n)
                for k in range(KD):
                    for i in range(NT):
                        ins = pe.matmul(bank[7 - k // 4][:, P * (k % 4):P * (k % 4) + P], xn2[:, i, P * k:P * k + P],
                                        select[:, i, :], start=(i == 0), stop=(i == NT - 1))
                ins.then_inc(gathered, 1)

            def slot_info(o, sel, done):
                for half in range(2):
                    for i in range(NT):
                        ins = pe.matmul(o[SLOTS * half:SLOTS * half + SLOTS, 0:2], sel[:, i, 0:SLOTS], expert_data[:, i, :],
                                        start=(i == 0), stop=(i == NT - 1), tile_position=(0, SLOTS * half))
                ins.then_inc(done, 1)

            def hidden_sums(xg, e, used=None):
                pe.wait_ge(b1_in, 16 * e + 16)
                for r in range(4):
                    half = r % 2
                    pe.matmul(bank[4 + r // 2][64 * half:64 * half + 64], ones[32 * r:32 * r + 1, 0:SLOTS],
                              exp_b1[32 * r:32 * r + 1, :], start=True, stop=False, tile_position=(32 * r, 64 * half))
                for n, k in enumerate(W1_ORDER):
                    pe.wait_ge(w1_in[k], 16 * e + 16)
                    for r in range(4):
                        half = r % 2
                        ins = pe.matmul(bank[4 + r // 2][64 * half:64 * half + 64], xg[:, k, 0:SLOTS],
                                        w1[k][:, 512 * r:512 * r + 512], start=False, stop=(n == KD - 1),
                                        tile_position=(0, 64 * half))
                    if used:
                        ins.then_inc(used, 1)
                return ins

            def turn_hidden(ready, n, done):
                pe.wait_ge(ready, n)
                for j in range(4):
                    ins = pe.transpose(bank[7][:, P * j:P * j + P], hidden[:, P * j:P * j + P], ident)
                ins.then_inc(done, 1)

            def output_sums(ready, n, e, used=None):
                pe.wait_ge(ready, n)
                for k in range(KD):
                    pe.wait_ge(w2_in[k], 16 * e + 16)
                    for half in range(2):
                        ins = pe.matmul(bank[6][64 * half:64 * half + 64], hiddenT[:, k % 4, 64 * (k // 4):64 * (k // 4) + 64],
                                        w2[k][:, 512 * half:512 * half + 512], start=(k == 0), stop=(k == KD - 1),
                                        tile_position=(0, 64 * half))
                    if used:
                        ins.then_inc(used, 1)
                return ins

            def spread_out(ready, n, matrix, y, done):
                pe.wait_ge(ready, n)
                for i in range(NT):
                    for half in range(2):
                        rows_ = slice(64 * half, 64 * half + 64)
                        ins = pe.matmul(bank[2 * i + half], matrix[rows_, P * i:P * i + P], y[rows_, :],
                                        start=False, stop=True, skip_group_check=True)
                ins.then_inc(done, 1)

            pe.wait_ge(route_ready, 1)
            gather(1)
            slot_info(bank[5], select, info_done)

            def expert(e, first=False):
                count = pe.value_load(counts_int_i[0:1, 0:1] if first else counts_int_i[0:1, bass.ds(e, 1)],
                                      min_val=0, max_val=T)
                before = pe.value_load(before_int_i[0:1, 0:1] if first else before_int_i[0:1, bass.ds(e, 1)],
                                       min_val=0, max_val=3 * N_EXP)
                pe.wait_ge(xg_lo, e + 1)
                pe.wait_ge(xg_hi, e + 1)
                pe.wait_ge(main_steps["slot_data"], e + 1)
                if not first:
                    pe.wait_ge(y_ready, e)
                def further_pass(p):
                    n = before + p
                    pe.wait_ge(ov["select"], n)
                    for k in range(KD):
                        for i in range(NT):
                            pe.matmul(bank[7][:, SLOTS * k:SLOTS * k + SLOTS], xn2[:, i, P * k:P * k + P],
                                      select_ov[:, i, :], start=(i == 0), stop=(i == NT - 1))
                    slot_info(bank[6], select_ov, ov["gathered"])
                    pe.wait_ge(ov["xg"], n)
                    hidden_sums(xgT_ov, e).then_inc(ov["hidden"], 1)
                    turn_hidden(ov["act"], n, ov["turned"])
                    output_sums(ov["copied"], n, e).then_inc(ov["y"], 1)
                    spread_out(ov["y_copied"], n, spreadT_ov, y_ov, ov["done"])

                with pe.If(count > SLOTS):
                    further_pass(1)
                    with pe.If(count > 2 * SLOTS):
                        further_pass(2)
                        with pe.If(count > 3 * SLOTS):
                            further_pass(3)
                hidden_sums(xgT, e, w1_used)
                if not first:
                    pe.wait_ge(spread_ready, e)
                    spread_out(y_ready, e, spreadT, y_sb, spread_done)
                gather(e + 2)
                pe.wait_ge(xg_lo, e + 2)
                turn_hidden(hidden_ready, e + 1, hidden_turned)
                slot_info(bank[5], select, info_done)
                pe.wait_ge(xg_hi, e + 2)
                output_sums(hiddenT_ready, e + 1, e, w2_used)

            pe.sem_inc(spread_done, 1)
            expert(0, first=True)
            with pe.Fori(1, N_EXP) as e:
                expert(e)
            pe.wait_ge(spread_ready, N_EXP)
            spread_out(y_ready, N_EXP, spreadT, y_sb, spread_done)

            pe.wait_ge(moe_out_ready, 1)
            for b in range(2):
                pe.sem_inc(ffn_used[b], 1)
            for n in range(n_jobs, first_even):
                run_job(n)
            for s in range(n_units, len(units) + 2):
                if s < len(units):
                    scores(s)
                for n in steps_b[s - n_units]:
                    run_job(n)
                if n_units < s <= len(units):
                    turn(s - 1)
                if s >= n_units + 2:
                    value(s - 2)
            for n in range(even_end, even_all_end):
                run_job(n)

            def ffn_sums_of(layer, b, n):
                pe.wait_ge(ffn_up_in[b], n * 32)
                w = ring[ffn_panels[layer][b] % 4][:, 0:2048].rearrange("p (g k n) -> p g k n", g=2, k=KD)
                for g in range(2):
                    for k in range(KD):
                        ins = pe.matmul(bank[4 + b][:, T * g:T * g + T], w[:, g, k, :], xT[:, k, :],
                                        start=(k == 0), stop=(k == KD - 1))
                ins.then_inc(ffn_sums[b], 1)

            def ffn_down(layer, b, n):
                pe.wait_ge(ffn_act[b], n)
                pe.wait_ge(ffn_down_in[b], n * 16)
                w = ring[ffn_panels[layer][b] % 4][:, 2048:3072]
                for i in range(NT):
                    for half in range(2):
                        ins = pe.matmul(bank[2 * i + half], ffn_h[:, b, P * i:P * i + P], w[:, 512 * half:512 * half + 512],
                                        start=False, stop=True, skip_group_check=True)
                ins.then_inc(ffn_used[b], 1)

            def feed_forward(layer, last_xt):
                empty(pe, last_xt)
                empty(pe, last_xt - 1)
                base = 11 * layer
                for i in range(NT):
                    for half in range(2):
                        residual(bank[2 * i + half], i, half)
                ffn_sums_of(layer, 0, base + 1)
                with pe.Fori(0, NF // 2 - 1) as e:
                    ffn_sums_of(layer, 1, e + base + 1)
                    ffn_down(layer, 0, e + base + 1)
                    ffn_sums_of(layer, 0, e + base + 2)
                    ffn_down(layer, 1, e + base + 1)
                ffn_sums_of(layer, 1, base + 11)
                ffn_down(layer, 0, base + 11)
                ffn_down(layer, 1, base + 11)

            feed_forward(0, even_all_end - 1)
            for n in range(even_all_end, len(jobs)):
                if n == even_all_end:
                    pe.wait_ge(z_ready, 2)
                run_job(n)
            feed_forward(1, len(jobs) - 1)

        @block.vector
        def _(dve):
            own = dve_own

            def chained(instruction):
                own.add(instruction)
                dve.wait_ge(own.sem, own.n)

            dve.wait_ge(const_in, 64)
            dve.memset(kcT, 0.0)
            dve.tensor_scalar(nsink, sinks, -1.0, None, ALU.mult)
            for n in range(2):
                ins = dve.tensor_tensor_reduce(score_sb[:, 64 * n:64 * n + 64], lam_row[:, 128 * n:128 * n + 64],
                                               lam_row[:, 128 * n + 64:128 * n + 128], 1.0, 0.0, ALU.mult, ALU.add,
                                               lam_sum[:, n:n + 1])
            ins.then_inc(lam_sums, 1)
            dve.wait_ge(rows_turned, 1)
            chained(dve.tensor_copy(cols, bank[2][:, 0:N_COLS]))
            g0 = ROW_B + BI_GATE
            dve.tensor_scalar(cols[:, g0:g0 + 24], cols[:, g0:g0 + 24], 0.5, None, ALU.mult).then_inc(cols_ready, 1)
            dve.wait_ge(silu_tanh, 1)
            dve.wait_ge(cols_ready, 1)
            chained(dve.scalar_tensor_tensor(silu_c, silu_c, 1.0, cols[:, ROW_C:ROW_C + 8], ALU.add, ALU.mult))
            dve.scalar_tensor_tensor(silu32, ones.rearrange("p (k n) -> p k n", k=8)[:, :, 0:1].to_broadcast([P, 8, 32]), 0.5,
                                     silu_c.rearrange("p (k o) -> p k o", o=1).to_broadcast([P, 8, 32]),
                                     ALU.mult, ALU.mult).then_inc(silu_ready, 1)
            dve.wait_ge(lam_exps, 1)
            dve.scalar_tensor_tensor(lam_neg, lam_sum[:, 3:4], -LAM_INIT, lam_sum[:, 2:3], ALU.add, ALU.subtract)
            for h in range(8):
                ins = dve.scalar_tensor_tensor(alibi[:, h, :], csc("dist"), 2.0 ** -(h + 1), csc("causal"),
                                               ALU.mult, ALU.add)
            chained(ins)
            dve.tensor_tensor(alibi_w[:, :, 0:128], alibi[:, :, 128:256],
                              csc("window").rearrange("p (o n) -> p o n", o=1).to_broadcast([P, 8, 128]), ALU.add)
            dve.tensor_copy(alibi_w[:, :, 128:256], alibi[:, :, 256:384])
            dve.wait_ge(std_ready, 1)
            chained(dve.reciprocal(rstd, rstd))
            for i in range(NT):
                ins = dve.tensor_scalar(xn[:, i, :], x_res[:, i, :], rstd[:, i:i + 1], None, ALU.mult)
            ins.then_inc(xn_ready, 1)

            def mod_columns(src, g):
                return dve.tensor_copy(mod[:, 16 * g:16 * g + 16].rearrange("p (r j) -> p r j", r=4),
                                       src.rearrange("p (j r x) -> p r j x", j=4, r=4)[:, :, :, 0])

            dve.wait_ge(modb_in, 64)
            dve.wait_ge(mod0_done, 4)
            dve.tensor_tensor(modrow[:, 0, :], modrow[:, 0, :], bank[3][:, :], ALU.add).then_inc(modrow_ready, 1)
            dve.wait_ge(mod_turned, 1)
            chained(mod_columns(bank[3][:, :], 0))
            dve.scalar_tensor_tensor(scale1, mod[:, 8:16], 1.0, cols[:, ROW_N1:ROW_N1 + 8], ALU.add,
                                     ALU.mult).then_inc(mod_ready, 1)
            dve.wait_ge(mod_ready, 1)
            for q in (1, 3):
                dve.wait_ge(x_turned, q + 1)
                for k in (2 * q, 2 * q + 1):
                    dve.tensor_scalar(hT[:, k, :], bank[4 + q][:, T * (k % 2):T * (k % 2) + T], scale1[:, k:k + 1],
                                      mod[:, k:k + 1], ALU.mult, ALU.add).then_inc(hT_dve, 1)

            def stats(u, s):
                return unit_stat[:, s, 2 * u:2 * u + 2]

            job_swaps = [n for n, jb in enumerate(jobs) if jb["kind"] == "swap"]

            def row_max(u):
                kind, j, i = units[u]
                nk = P * (i + 1)
                dve.wait_ge(scores_done, u + 1)
                if u >= 2:
                    dve.wait_ge(exp_done, u - 1)
                src = score_banks[:, :, 0:nk]
                s = score_sb[:, 512 * (u % 2):512 * (u % 2) + 512].rearrange("p (h n) -> p h n", h=2)[:, :, 0:nk]
                lo = 0 if i == 0 else P
                if kind == "diff":
                    add = alibi[:, 2 * j + 1:2 * j + 2, lo:lo + nk].to_broadcast([P, 2, nk])
                elif kind == "dilated":
                    add = toep[:, 2 * j:2 * j + 2, lo:lo + nk]
                elif kind == "window" and i == 1:
                    add = alibi_w[:, j::4, :]
                else:
                    add = alibi[:, j::4, lo:lo + nk]
                chained(dve.scalar_tensor_tensor(s, src, HD ** -0.5, add, ALU.mult, ALU.add))
                ins = dve.tensor_reduce(stats(u, 0), s, AX.X, ALU.max, negate=True)
                if kind == "window":
                    chained(ins)
                    chained(dve.tensor_tensor(stats(u, 0), stats(u, 0), nsink[:, j::4], ALU.min))
                    ins = dve.tensor_tensor(stats(u, 2), stats(u, 0), sinks[:, j::4], ALU.add)
                ins.then_inc(max_done, 1)

            def normalize(u):
                kind, j, i = units[u]
                nk = P * (i + 1)
                dve.wait_ge(exp_done, u + 1)
                r = stats(u, 1)
                if kind == "window":
                    chained(dve.tensor_tensor(r, r, stats(u, 2), ALU.add))
                chained(dve.reciprocal(r, r))
                if kind in ("select", "local"):
                    which = 1 if kind == "select" else 2
                    g = nsa_g[:, i, 3 * j + which::12]
                    chained(dve.tensor_tensor(r, r, g, ALU.mult))
                if kind == "diff":
                    chained(dve.tensor_tensor(r[:, 1:2], r[:, 1:2], lam_neg, ALU.mult))
                at = 512 * (u % 2)
                ins = dve.tensor_scalar(prob[:, at:at + nk], prob[:, at:at + nk], r[:, 0:1], None, ALU.mult)
                second = prob[:, at + 256:at + 256 + nk]
                if kind == "diff":
                    chained(ins)
                    ins = dve.scalar_tensor_tensor(prob[:, at:at + nk], second, r[:, 1:2], prob[:, at:at + nk],
                                                   ALU.mult, ALU.add)
                else:
                    ins = dve.tensor_scalar(second, second, r[:, 1:2], None, ALU.mult)
                ins.then_inc(norm_done, 1)

            unfinished = []

            def finish_conv():
                if unfinished:
                    m = jobs[unfinished.pop()]
                    o_ = m["order"]
                    dve.wait_ge(conv_tanh, o_ + 1)
                    dve.scalar_tensor_tensor(qkT[:, m["block"], :], conv_t[:, o_ % 2, :], 1.0, conv_acc[:, o_ % 2, :],
                                             ALU.add, ALU.mult).then_inc(conv_done, 1)

            def empty_job(n):
                jb = jobs[n]
                if jb["kind"] != "conv":
                    finish_conv()
                if jb["engine"] != "dve":
                    return
                kind, src = jb["kind"], bank[n % 2]
                dve.wait_ge(job_done, n + 1)
                if kind == "token":
                    m = 128 if jb["gates"] else jb["n"]
                    ins = dve.tensor_copy(vtok[:, jb["tile"], jb["dest"]:jb["dest"] + m], src[:, 0:m])
                    if jb["gates"]:
                        ins = dve.tensor_copy(nsa_g[:, jb["tile"], :], src[:, 128:152])
                elif kind == "cmp_hidden":
                    h, ht = hid[0:64, :], hid_t[0:64, :]
                    dve.tensor_copy(h, src[0:64, 0:256]).then_inc(job_empty["dve"], 1)
                    empty(dve, n)
                    chained(dve.tensor_tensor(ht, h, h, ALU.mult))
                    chained(dve.tensor_scalar(ht, ht, 0.044715, 1.0, ALU.mult, ALU.add))
                    dve.tensor_tensor(ht, ht, h, ALU.mult).then_inc(gelu_in, 1)
                    dve.wait_ge(gelu_tanh, 1)
                    chained(dve.scalar_tensor_tensor(h, ht, 1.0, h, ALU.add, ALU.mult))
                    dve.tensor_scalar(h, h, 0.5, None, ALU.mult).then_inc(hid_ready, 1)
                    dve.wait_ge(nsa_tanh, 1)
                    flat_g = nsa_g.rearrange("p a b -> p (a b)")
                    chained(dve.tensor_scalar(flat_g, flat_g, 1.0, 0.5, ALU.add, ALU.mult))
                    ins = None
                elif kind == "cmp_v_rep":
                    chained(dve.tensor_copy(vrep, src[:, 0:64]))
                    ins = dve.tensor_tensor(vz, vrep.rearrange("p (o d) -> p o d", o=1).to_broadcast([P, 8, 64]),
                                            cmp_head.rearrange("p (h o) -> p h o", o=1).to_broadcast([P, 8, 64]),
                                            ALU.mult)
                elif kind == "cmp_scores":
                    s = cmp_s.rearrange("p (a c) -> p a c", c=16)
                    st, rs, g = cmp_stat[:, 0:16], cmp_stat[:, 16:32], cmp_stat[:, 32:48]

                    def wide(v):
                        return v.rearrange("p (a o) -> p a o", o=1).to_broadcast([P, 16, 16])

                    dve.scalar_tensor_tensor(cmp_s, src[:, 0:T], HD ** -0.5, ca("cmp_add"), ALU.mult,
                                             ALU.add).then_inc(job_empty["dve"], 1)
                    empty(dve, n)
                    chained(dve.tensor_reduce(st, s, AX.X, ALU.max))
                    dve.tensor_tensor(s, s, wide(st), ALU.subtract).then_inc(cmp_exp_in, 1)
                    dve.wait_ge(cmp_exp, 1)
                    chained(dve.tensor_reduce(rs, s, AX.X, ALU.add))
                    chained(dve.reciprocal(rs, rs))
                    chained(dve.tensor_tensor(g.rearrange("p (i h) -> p i h", i=2), rs.rearrange("p (i h) -> p i h", i=2),
                                              nsa_g[:, :, 0::3], ALU.mult))
                    chained(dve.tensor_tensor(s, s, wide(g), ALU.mult))
                    dve.tensor_tensor(cmp_s, cmp_s, ca("cmp_valid"), ALU.mult).then_inc(cmp_prob_ready, 1)
                    ins = None
                elif kind == "mod":
                    g = jb["group"]
                    ins = dve.tensor_tensor(modrow[:, g, :], modrow[:, g, :], src[:, :], ALU.add)
                elif kind == "mod_t":
                    ins = mod_columns(src[:, :], jb["group"])
                elif kind == "branch":
                    k, br = jb["chunk"], jb["branch"]
                    gate = gateT[:, 8 * br + k, :]
                    if br == 0:
                        ins = dve.scalar_tensor_tensor(mergedT[:, k, :], gate, 1.0, src[:, 0:T], ALU.add, ALU.mult)
                    else:
                        chained(dve.scalar_tensor_tensor(score_sb[:, 0:T], gate, 1.0, src[:, 0:T], ALU.add, ALU.mult))
                        ins = dve.tensor_tensor(mergedT[:, k, :], mergedT[:, k, :], score_sb[:, 0:T], ALU.add)
                elif kind == "mix_out":
                    part = slice(512 * jb["half"], 512 * jb["half"] + 512)
                    if jb["half"] == 0 and jb["tile"] == 0:
                        empty(dve, job_g1 + 3)
                    chained(dve.tensor_tensor(score_sb[:, 0:512], src[:, :], g1b[:, part], ALU.mult))
                    ins = dve.tensor_tensor(x_res[:, jb["tile"], part], x_res[:, jb["tile"], part],
                                            score_sb[:, 0:512], ALU.add)
                elif kind == "xt" or kind == "y_turn":
                    for k in (2 * jb["quarter"], 2 * jb["quarter"] + 1):
                        dest = (xT if kind == "xt" else yT)[:, k, :]
                        part = src[:, T * (k % 2):T * (k % 2) + T]
                        if kind == "y_turn":
                            ins = dve.tensor_scalar(dest, part, 0.5, None, ALU.mult)
                        elif jb["b"] is None:
                            ins = dve.tensor_scalar(dest, part, col(jb["g"] + k), None, ALU.mult)
                        else:
                            ins = dve.tensor_scalar(dest, part, col(jb["g"] + k), col(jb["b"] + k), ALU.mult, ALU.add)
                elif kind == "b_token":
                    ins = dve.tensor_copy(jb["dest"], src[:, 0:512])
                elif kind == "swap":
                    if n != job_swaps[0]:
                        dve.wait_ge(job_empty["dve"], emptied[job_swaps[job_swaps.index(n) - 1]])
                    m = jb["m"]
                    dve.tensor_tensor(rot[:, m, :], raw[:, m, :], cbc("cos"), ALU.mult)
                    chained(dve.tensor_tensor(rot_sin, src[:, 0:T], cbc("sin"), ALU.mult))
                    ins = dve.tensor_tensor(rot[:, m, :], rot[:, m, :], rot_sin, ALU.add)
                elif kind == "ret_scores":
                    h = jb["head"]
                    ins = dve.tensor_tensor(decayed[:, h, :], src[:, 0:384], cbc("decay")[:, 384 * h:384 * h + 384], ALU.mult)
                elif kind == "conv":
                    o_, c = jb["order"], COL_O + jb["block"]
                    acc = conv_acc[:, o_ % 2, :]
                    if o_ >= 2:
                        dve.wait_ge(conv_done, o_ - 1)
                    chained(dve.tensor_scalar(acc, src[:, 0:T], col(c + 48), None, ALU.mult))
                    for lag in (1, 2, 3):
                        ins = dve.scalar_tensor_tensor(acc[:, lag:T], src[:, 0:T - lag], col(c + 48 - 16 * lag),
                                                       acc[:, lag:T], ALU.mult, ALU.add)
                        if lag < 3:
                            chained(ins)
                elif kind == "gates":
                    dve.tensor_copy(gates_o.rearrange("p a b -> p (a b)"), src[:, 0:16]).then_inc(job_empty["dve"], 1)
                    empty(dve, n)
                    zf = gates_o[:, :, 4:8]
                    dve.scalar_tensor_tensor(log_f, zf, -1.0, zf, ALU.mult, ALU.max).then_inc(abs_ready, 1)
                    dve.wait_ge(exp_abs_ready, 1)
                    dve.scalar_tensor_tensor(log_f, zf, 0.0, log_f, ALU.min, ALU.subtract).then_inc(log_f_ready, 1)
                    ins = None
                elif kind == "cumsum":
                    chained(dve.tensor_copy(cum_f.rearrange("p a b -> p (a b)"), src[:, 0:8]))
                    ins = dve.tensor_tensor(low_i, gates_o[:, :, 0:4], cum_f, ALU.subtract)
                elif kind == "row_spread":
                    h = jb["head"]
                    dve.tensor_tensor(expD[:, h, 0:P], src[:, 0:P], cbc("causal_b")[:, 0:P], ALU.add)
                    ins = dve.tensor_tensor(expD[:, h, P:3 * P], src[:, 0:T], cbc("causal_b")[:, P:3 * P], ALU.add)
                elif kind == "ml_scores":
                    u = jb["u"]
                    h, i = units_o[u]
                    if u == 0:
                        dve.wait_ge(e_ready, 1)
                    nk = P * (i + 1)
                    dve.tensor_tensor_reduce(prob[:, 512 * (u % 2):512 * (u % 2) + nk], src[:, 0:nk],
                                             expD[:, h, P * i:P * i + nk], 0.25 / 16.0, 0.0, ALU.mult, ALU.add,
                                             den_r[:, u:u + 1]).then_inc(job_empty["dve"], 1)
                    empty(dve, n)
                    den = den_r[:, u:u + 1]
                    chained(dve.scalar_tensor_tensor(den, den, -1.0, den, ALU.mult, ALU.max))
                    chained(dve.tensor_tensor(den, den, floor_e[:, i, h:h + 1], ALU.max))
                    chained(dve.reciprocal(den, den))
                    ins = None
                elif kind == "ml_value":
                    u = jb["u"]
                    h, i = units_o[u]
                    ins = dve.tensor_scalar(y_odd[:, i, T * h:T * h + T], src[:, 0:T], den_r[:, u:u + 1], None, ALU.mult)
                if ins is not None:
                    ins.then_inc(job_empty["dve"], 1)
                if kind == "conv":
                    finish_conv()
                    unfinished.append(n)
                if kind == "row_spread" and jb["head"] == 3:
                    empty(dve, n)
                    dve.tensor_reduce(neg_r[:, 0, :], expD[:, :, 0:P], AX.X, ALU.max, negate=True)
                    chained(dve.tensor_reduce(neg_r[:, 1, :], expD[:, :, P:3 * P], AX.X, ALU.max, negate=True))
                    chained(dve.tensor_scalar(neg_r, neg_r, 0.0, None, ALU.min))
                    dve.tensor_tensor(floor_e, neg_r, cum_f, ALU.subtract).then_inc(e_in, 1)
                if kind in ("branch", "mix_out"):
                    dve.wait_ge(job_empty["dve"], emptied[n])

            def build_cmp_in():
                for n in range(4):
                    kv, g = n // 2, n % 2
                    v = shifted[:, n, :]
                    src = bass.AP(tensor=v.tensor, offset=v.offset, ap=[v.ap[0], [2, 16], [16, 15]])
                    at = ROW_POS + 16 * kv
                    dve.tensor_tensor(cmp_in[:, kv, :, 15 * g:15 * g + 15], src,
                                      cols[:, at:at + 16].rearrange("p (m o) -> p m o", o=1).to_broadcast([P, 16, 15]),
                                      ALU.add)
                dve.memset(cmp_in[:, :, :, 30:32], 0.0).then_inc(cmp_ready, 1)

            for n in range(first_a):
                empty_job(n)
            for s in range(n_units + 2):
                if s < n_units:
                    row_max(s)
                for n in steps[s]:
                    if n == job_hid:
                        empty(dve, job_last_shift)
                        build_cmp_in()
                    empty_job(n)
                if s < n_units:
                    normalize(s)
            dve.wait_ge(diff_std, 1)
            chained(dve.reciprocal(sub_stat, sub_stat))
            for i in range(NT):
                o = o_tok[:, i, :].rearrange("p (h e) -> p h e", h=4)
                ins = dve.scalar_tensor_tensor(o, o, 1.0 - LAM_INIT,
                                               sub_stat[:, 4 * i:4 * i + 4].rearrange("p (h o) -> p h o", o=1)
                                               .to_broadcast([P, 4, P]), ALU.mult, ALU.mult)
            ins.then_inc(diff_ready, 1)
            for n in range(steps_end, n_jobs):
                empty_job(n)

            dve.wait_ge(std2_ready, 1)
            chained(dve.reciprocal(rstd, rstd))
            for i in range(NT):
                ins = dve.tensor_scalar(xn2[:, i, :], x_res[:, i, :], rstd[:, i:i + 1], None, ALU.mult)
            own.add(ins)
            dve.scalar_tensor_tensor(scale2, mod[:, 32:40], 1.0, cols[:, ROW_N2:ROW_N2 + 8], ALU.add,
                                     ALU.mult).then_inc(xn2_ready, 1)
            dve.wait_ge(xn2_ready, 1)
            for q in (1, 3):
                dve.wait_ge(x2_turned, q + 1)
                for k in (2 * q, 2 * q + 1):
                    dve.tensor_scalar(h2T[:, k, :], bank[2 + q][:, T * (k % 2):T * (k % 2) + T], scale2[:, k:k + 1],
                                      mod[:, 24 + k:25 + k], ALU.mult, ALU.add).then_inc(h2T_dve, 1)
            dve.wait_ge(bias_row_done, 1)
            dve.tensor_copy(bias_row[0:8, :], bank[1][0:8, 0:384]).then_inc(bias_row_ready, 1)
            dve.memset(slot_of[:, :, N_EXP:N_EXP + 1], -1.0)
            dve.memset(id_gate[:, :, N_EXP:N_EXP + 1, :], 0.0)
            for i in range(NT):
                dve.tensor_copy(id_gate[:, i, 0:N_EXP, 0], ca("token_id")[:, i:i + 1].to_broadcast([P, N_EXP]))
            dve.wait_ge(logits_done, 1)
            chained(dve.tensor_copy(logits.rearrange("p a b -> p (a b)"), bank[6][:, 0:64]))
            for i in range(NT):
                ins = dve.max(best[:, i, :], logits[:, i, :])
            chained(ins)
            dve.tensor_scalar(top_stat[:, 0:2], best[:, :, 0], -1.0, None, ALU.mult).then_inc(top_ready, 1)
            for i in range(NT):
                ins = dve.max_index(best_at_int.bitcast(U32)[:, i, :], best[:, i, :], logits[:, i, :])
            chained(ins)
            chained(dve.tensor_copy(best_at, best_at_int.bitcast(U32)))
            for i in range(NT):
                chained(dve.tensor_tensor(onehots[:, i], iota[:, 0:32].rearrange("p (o e) -> p o e", o=1).to_broadcast([P, 4, 32]),
                                          best_at[:, i, 0:TOP_K].rearrange("p (k o) -> p k o", o=1).to_broadcast([P, 4, 32]),
                                          ALU.is_equal))
                ins = dve.tensor_reduce(chosen[:, i, :], onehots[:, i].rearrange("p k e -> p e k"), AX.X, ALU.add)
            chained(ins)
            dve.wait_ge(top_exp, 1)
            chained(dve.reciprocal(top_stat[:, 2:4], top_stat[:, 2:4]))
            for i in range(NT):
                chained(dve.tensor_scalar(top_gate[:, i, :], top_gate[:, i, :], top_stat[:, 2 + i:3 + i], None, ALU.mult))
                chained(dve.tensor_tensor(onehots[:, i], onehots[:, i],
                                          top_gate[:, i, :].rearrange("p (k o) -> p k o", o=1).to_broadcast([P, 4, 32]),
                                          ALU.mult))
                ins = dve.tensor_reduce(gates_t[:, i, :], onehots[:, i].rearrange("p k e -> p e k"), AX.X, ALU.add)
            ins.then_inc(chosen_ready, 1)
            dve.wait_ge(chosen_ready, 1)
            chained(dve.tensor_copy(id_gate[:, :, 0:N_EXP, 1], gates_t))
            dve.wait_ge(places_done, 1)
            dve.tensor_copy(gatesT[0:N_EXP, :], bank[7][0:N_EXP, P:P + T]).then_inc(gatesT_ready, 1)
            place = bank[7][:, 0:64].rearrange("p (i e) -> p i e", i=2)
            chained(dve.scalar_tensor_tensor(slot_of[:, :, 0:N_EXP], place, 1.0, chosen, ALU.add, ALU.mult))
            dve.tensor_scalar(slot_of[:, :, 0:N_EXP], slot_of[:, :, 0:N_EXP], -1.0, None, ALU.add)
            chained(dve.tensor_copy(counts[:, 0:N_EXP], bank[7][:, 64:96]))
            for p in range(1, T // SLOTS):
                ins = dve.tensor_scalar(passes[:, p - 1, :], counts[:, 0:N_EXP], float(p * SLOTS), None, ALU.is_gt)
            dve.tensor_copy(counts_int_i, counts[:, 0:N_EXP])
            chained(ins)
            chained(dve.tensor_tensor(passes[:, 0, :], passes[:, 0, :], passes[:, 1, :], ALU.add))
            chained(dve.tensor_tensor(passes[:, 0, :], passes[:, 0, :], passes[:, 2, :], ALU.add))
            chained(dve.tensor_tensor_scan(passes[:, 1, :], passes[:, 0, :], passes[:, 0, :], 0.0, ALU.add, ALU.bypass))
            chained(dve.tensor_tensor(passes[:, 2, :], passes[:, 1, :], passes[:, 0, :], ALU.subtract))
            dve.tensor_copy(before_int_i, passes[:, 2, :]).then_inc(route_ready, 1)

            def make_select(n, done):
                data = id_gate[:, :, 0, :] if isinstance(n, int) else id_gate[:, :, bass.ds(n, 1), :].rearrange("p i o c -> p i (o c)")
                dve.tensor_copy(expert_data, data)
                for i in range(NT):
                    where = slot_of[:, i, 0:1] if isinstance(n, int) else slot_of[:, i, bass.ds(n, 1)]
                    ins = dve.tensor_scalar(select[:, i, :], iota[:, 0:P], where, None, ALU.is_equal)
                ins.then_inc(done, 1)

            def spread_matrix(matrix, data, done):
                dve.tensor_scalar(matrix, iota, data[:, 0:1], data[:, 1:2], ALU.is_equal, ALU.mult).then_inc(done, 1)

            def activation(hidden_sem, gate_sem, tanh_sem, ready_sem, own_steps, n, sums):
                dve.wait_ge(hidden_sem, sums)
                dve.tensor_scalar(gate_part, bank[4], 7.0, None, ALU.min).then_inc(gate_sem, 1)
                dve.tensor_scalar(up_part, bank[5], 7.0, -7.0, ALU.min, ALU.max).then_inc(own_steps["clipped"], 1)
                dve.wait_ge(gate_sem, n)
                dve.wait_ge(own_steps["clipped"], n)
                dve.scalar_tensor_tensor(up_part, up_part, 1.0, gate_part, ALU.add,
                                         ALU.mult).then_inc(own_steps["up_times_gate"], 1)
                dve.wait_ge(own_steps["up_times_gate"], n)
                dve.wait_ge(tanh_sem, n)
                dve.scalar_tensor_tensor(hidden, gate_tanh, 1.0, up_part, ALU.add, ALU.mult).then_inc(ready_sem, 1)

            def copy_gathered(n):
                dve.wait_ge(gathered, n)
                for k in range(4, KD):
                    ins = dve.tensor_scalar(xgT[:, k, :], bank[6][:, P * (k - 4):P * (k - 4) + P], scale2[:, k:k + 1],
                                            mod[:, 24 + k:25 + k], ALU.mult, ALU.add)
                ins.then_inc(xg_hi, 1)

            dve.wait_ge(route_ready, 1)
            make_select(0, select_ready)
            copy_gathered(1)
            dve.wait_ge(info_done, 1)
            dve.tensor_copy(slot_data, bank[5][:, 0:2]).then_inc(main_steps["slot_data"], 1)
            with dve.Fori(0, N_EXP) as e:
                count = dve.value_load(counts_int_i[0:1, bass.ds(e, 1)], min_val=0, max_val=T)
                before = dve.value_load(before_int_i[0:1, bass.ds(e, 1)], min_val=0, max_val=3 * N_EXP)
                def further_pass(p):
                    n = before + p
                    for i in range(NT):
                        ins = dve.tensor_scalar(select_ov[:, i, :], iota[:, SLOTS * p:SLOTS * p + SLOTS],
                                                slot_of[:, i, bass.ds(e, 1)], None, ALU.is_equal)
                    ins.then_inc(ov["select"], 1)
                    dve.wait_ge(ov["gathered"], n)
                    wide = [P, KD, SLOTS]
                    dve.tensor_tensor(xgT_ov, bank[7].rearrange("p (k s) -> p k s", k=KD),
                                      scale2.rearrange("p (k o) -> p k o", o=1).to_broadcast(wide),
                                      ALU.mult).then_inc(more_steps["scaled"], 1)
                    dve.wait_ge(more_steps["scaled"], n)
                    dve.tensor_tensor(xgT_ov, xgT_ov, mod[:, 24:32].rearrange("p (k o) -> p k o", o=1).to_broadcast(wide),
                                      ALU.add)
                    dve.tensor_copy(slot_data_ov, bank[6][:, 0:2]).then_inc(more_steps["slot_data"], 1)
                    dve.wait_ge(more_steps["slot_data"], n)
                    spread_matrix(spreadT_ov, slot_data_ov, ov["xg"])
                    activation(ov["hidden"], ov["gate"], ov["tanh"], ov["act"], more_steps, n, n)
                    dve.wait_ge(ov["done"], n)
                    dve.nop(nofuse=True)

                with dve.If(count > SLOTS):
                    further_pass(1)
                    with dve.If(count > 2 * SLOTS):
                        further_pass(2)
                        with dve.If(count > 3 * SLOTS):
                            further_pass(3)
                make_select(e + 1, select_ready)
                activation(w1_used, gate_ready, tanh_ready, hidden_ready, main_steps, e + 1, e * KD + KD)
                copy_gathered(e + 2)
                dve.wait_ge(spread_done, e + 1)
                dve.wait_ge(main_steps["slot_data"], e + 1)
                spread_matrix(spreadT, slot_data, spread_ready)
                dve.wait_ge(info_done, e + 2)
                dve.wait_ge(spread_ready, e + 1)
                dve.tensor_copy(slot_data, bank[5][:, 0:2]).then_inc(main_steps["slot_data"], 1)
            dve.wait_ge(spread_done, N_EXP + 1)
            for i in range(NT):
                for half in range(2):
                    part = slice(512 * half, 512 * half + 512)
                    chained(dve.tensor_tensor(gate_part, bank[2 * i + half], g2b[:, part], ALU.mult))
                    chained(dve.tensor_tensor(x_res[:, i, part], x_res[:, i, part], gate_part, ALU.add))
            dve.sem_inc(moe_out_ready, 1)
            dve.wait_ge(x2_std, 1)
            chained(dve.reciprocal(rstd, rstd))
            dve.tensor_scalar(alpha_ident, ident, ALPHA, None, ALU.mult)
            for i in range(NT):
                dve.tensor_scalar(z[:, i, :], x_res[:, i, :], rstd[:, i:i + 1], None, ALU.mult).then_inc(z_normed, 1)
            dve.wait_ge(bias_in_b, 32)
            dve.wait_ge(consts_b_in, 16)
            chained(dve.tensor_tensor(toep, toep, cbc("log_mult").rearrange("p (o n) -> p o n", o=1)
                                      .to_broadcast([P, 8, 384]), ALU.add))
            for n in range(n_jobs, first_even):
                empty_job(n)
            for s in range(n_units, len(units) + 2):
                if s < len(units):
                    row_max(s)
                for n in steps_b[s - n_units]:
                    empty_job(n)
                if s < len(units):
                    normalize(s)
            dve.wait_ge(job_empty["act"], emptied[job_gr])
            for i in range(NT):
                for h in range(4):
                    ins = dve.bn_stats(ret_bn[:, 4 * i + h, :], y_even[:, i, P * h:P * h + P])
            chained(ins)
            for n in range(8):
                ins = dve.bn_aggr(ret_mv[:, n, :], ret_bn[:, n, :])
            chained(ins)
            dve.tensor_scalar(ret_mv[:, :, 1], ret_mv[:, :, 1], EPS, None, ALU.add).then_inc(ret_var, 1)
            chained(dve.scalar_tensor_tensor(g_tanh, g_tanh, 1.0, g_raw, ALU.add, ALU.mult))
            dve.wait_ge(ret_std, 1)
            chained(dve.reciprocal(ret_mv[:, :, 1], ret_mv[:, :, 1]))
            for i in range(NT):
                for h in range(4):
                    n = 4 * i + h
                    y_ = y_even[:, i, P * h:P * h + P]
                    ins = dve.tensor_scalar(y_, y_, ret_mv[:, n, 0:1], ret_mv[:, n, 1:2], ALU.subtract, ALU.mult)
            chained(ins)
            dve.scalar_tensor_tensor(y_even, y_even, 0.5, g_tanh, ALU.mult, ALU.mult).then_inc(ret_ready, 1)
            for n in range(even_end, even_mix_end):
                empty_job(n)

            def layer_norm(g, wait_tile, normed):
                for i in range(NT):
                    wait_tile(i)
                    for half in range(2):
                        ins = dve.bn_stats(ln_bn[:, 2 * i + half, :], z[:, i, 512 * half:512 * half + 512])
                    chained(ins)
                    chained(dve.bn_aggr(ln_mv[:, i, :], ln_bn[:, 2 * i:2 * i + 2, :]))
                    dve.tensor_scalar(ln_mv[:, i, 1:2], ln_mv[:, i, 1:2], EPS, None, ALU.add).then_inc(z_var, 1)
                    dve.wait_ge(z_std, 2 * g + i + 1)
                    chained(dve.reciprocal(ln_mv[:, i, 1:2], ln_mv[:, i, 1:2]))
                    dve.tensor_scalar(z[:, i, :], z[:, i, :], ln_mv[:, i, 0:1], ln_mv[:, i, 1:2], ALU.subtract,
                                      ALU.mult).then_inc(normed, 1)

            def ffn_conv_and_gate(layer, b, n, chunk):
                def weight(lag):
                    if isinstance(chunk, int):
                        at = COL_F[layer] + NF * lag + chunk
                        return cols[:, at:at + 1]
                    return cols[:, bass.ds(chunk + (COL_F[layer] + NF * lag), 1)]

                gate, up, acc, step = bank[4 + b][:, 0:T], bank[4 + b][:, T:2 * T], ffn_z[:, b, :], ffn_step[b]
                dve.wait_ge(ffn_sums[b], n)
                dve.tensor_scalar(acc, gate, weight(2), weight(3), ALU.mult, ALU.add).then_inc(step, 1)
                dve.wait_ge(step, n * 3 - 2)
                dve.scalar_tensor_tensor(acc[:, 1:T], gate[:, 0:T - 1], weight(1), acc[:, 1:T], ALU.mult,
                                         ALU.add).then_inc(step, 1)
                dve.wait_ge(step, n * 3 - 1)
                dve.scalar_tensor_tensor(acc[:, 2:T], gate[:, 0:T - 2], weight(0), acc[:, 2:T], ALU.mult,
                                         ALU.add).then_inc(ffn_conv[b], 1)
                dve.wait_ge(ffn_tanh[b], n)
                dve.wait_ge(ffn_used[b], n)
                dve.scalar_tensor_tensor(ffn_h[:, b, :], ffn_t[:, b, :], 1.0, acc, ALU.add, ALU.mult).then_inc(step, 1)
                dve.wait_ge(step, n * 3)
                dve.scalar_tensor_tensor(ffn_h[:, b, :], up, 0.5, ffn_h[:, b, :], ALU.mult,
                                         ALU.mult).then_inc(ffn_act[b], 1)

            def feed_forward(layer):
                with dve.Fori(0, NF // 2) as e:
                    for b in range(2):
                        ffn_conv_and_gate(layer, b, e + 11 * layer + 1, e * 2 + b)

            layer_norm(0, lambda i: empty(dve, job_mix0 + 2 * i + 1), z_normed)
            for n in range(even_mix_end, even_all_end):
                empty_job(n)
            feed_forward(0)
            layer_norm(1, lambda i: dve.wait_ge(z_ready, i + 1), z_normed)
            for n in range(even_all_end, job_yt[0]):
                empty_job(n)
            for i in range(NT):
                if i == 0:
                    empty(dve, job_yt[0] - 1)
                    empty(dve, job_o_last)
                dve.scalar_tensor_tensor(y_odd[:, i, :], o_tanh[:, i, :], 1.0, y_odd[:, i, :], ALU.add,
                                         ALU.mult).then_inc(y_odd_ready, 1)
            for n in range(job_yt[0], odd_mix_end):
                empty_job(n)
            layer_norm(2, lambda i: empty(dve, job_mix1 + 2 * i + 1), z_normed)
            for n in range(odd_mix_end, len(jobs)):
                empty_job(n)
            feed_forward(1)
            layer_norm(3, lambda i: dve.wait_ge(z_ready, i + 3), z_normed)
            dve.wait_ge(final_in, 32)
            for i in range(NT):
                dve.wait_ge(z_normed, 8 + i + 1)
                chained(dve.tensor_tensor(z[:, i, :], z[:, i, :], final_gb[:, 0, :], ALU.mult))
                dve.tensor_tensor(z[:, i, :], z[:, i, :], final_gb[:, 1, :], ALU.add).then_inc(tile_ready, 1)


INPUTS = ["x", "c", "mod_w", "mod_b", "norm1_g", "norm2_g", "w_in", "b_in", "sinks", "diff_lambda", "diff_subln_g",
          "cmp_pos", "cmp_w1", "cmp_b1", "cmp_w2", "cmp_b2", "w_branch", "w_out", "router_w", "router_b", "exp_w1",
          "exp_b1", "exp_w2", "exp_b2", "final_g", "even_w_in_2", "even_w_out_2", "rel_bias_2", "odd_w_in_2",
          "odd_gate_b_2", "odd_conv_w_2", "odd_w_out_2", "ffn_w_up_2", "ffn_conv_w_2", "ffn_conv_b_2",
          "ffn_w_down_2", "ln_g_2", "ln_b_2"]


def kernel(**inputs):
    import concourse.bacc as bacc
    from concourse.bass_utils import run_bass_kernel_spmd

    nc = bacc.Bacc("TRN2", target_bir_lowering=False, num_devices=1)
    arrays, a = {}, {}
    for name in INPUTS:
        arrays["in_" + name] = np.ascontiguousarray(inputs[name])
    for name, value in zip(("const_a", "const_s", "const_b", "onehot"), shape_constants()):
        arrays["in_" + name] = value
    for name, value in arrays.items():
        a[name[3:]] = nc.dram_tensor(name, value.shape, mybir.dt.from_np(value.dtype), kind="ExternalInput").ap()
    out = nc.dram_tensor("out_x", (1, T, D), F32, kind="ExternalOutput").ap()
    program(nc, a, out)
    r = run_bass_kernel_spmd(nc, [arrays], core_ids=[0])
    return r.results[0]["out_x"]
```
